# Optimizing a Trainium2 kernel written in Bass

```python
import math
import jax
import jax.numpy as jnp
from jax import lax
import numpy as np

D_MODEL = 1024
BATCH = 1
SEQ = 256
DEPTH = 2

GRID_W = 64
CTX_LEN = 256
EPS = 1e-6
ROPE_BASE = 10000.0
QBLOCK = 128
N_MOD = 6

MLA_HEADS = 4
MLA_Q_RANK = 256
MLA_KV_RANK = 128
MLA_NOPE = 64
MLA_ROPE = 32
MLA_V = 64
MLA_SCALE = (MLA_NOPE + MLA_ROPE) ** -0.5

SWA_HEADS = 4
SWA_KV_HEADS = 2
SWA_HEAD_DIM = 64
SWA_WINDOW = 128
SWA_SCALE = SWA_HEAD_DIM ** -0.5

DIFF_HEADS = 4
DIFF_QK = 32
DIFF_V = 64
DIFF_SCALE = DIFF_QK ** -0.5

POOL_WINDOWS = (2, 4, 8, 16)
POOL_GROUP = 64

MIX_A = MLA_HEADS * MLA_V
MIX_B = SWA_HEADS * SWA_HEAD_DIM
MIX_C = DIFF_HEADS * DIFF_V
MIX_D = len(POOL_WINDOWS) * POOL_GROUP
D_MIX = MIX_A + MIX_B + MIX_C + MIX_D

IN_SIZES = (MLA_Q_RANK, MLA_KV_RANK, MLA_ROPE,
            SWA_HEADS * SWA_HEAD_DIM, SWA_KV_HEADS * SWA_HEAD_DIM, SWA_KV_HEADS * SWA_HEAD_DIM,
            2 * DIFF_HEADS * DIFF_QK, 2 * DIFF_HEADS * DIFF_QK, DIFF_HEADS * DIFF_V,
            MIX_D)
D_IN = sum(IN_SIZES)

N_EXPERT_GROUPS = 4
EXPERTS_PER_GROUP = 4
N_EXPERTS = N_EXPERT_GROUPS * EXPERTS_PER_GROUP
TOP_K_IN_GROUP = 2
D_EXPERT = 512

kernel_name = "hybrid_headgroup_dit_hmoe"

def rms_norm(x, g):
    xf = x.astype(jnp.float32)
    y = xf * lax.rsqrt(jnp.mean(xf * xf, axis=-1, keepdims=True) + EPS)
    return (y * g.astype(jnp.float32)).astype(x.dtype)

def modulate(h, shift, scale):
    return h * (1 + scale) + shift

def axial_rope_table(length, dim):
    rows = length // GRID_W
    row = jnp.repeat(jnp.arange(rows), GRID_W).astype(jnp.float32)
    col = jnp.tile(jnp.arange(GRID_W), rows).astype(jnp.float32)
    n = dim // 4
    inv = ROPE_BASE ** (-jnp.arange(n, dtype=jnp.float32) / n)
    ang = jnp.concatenate([row[:, None] * inv, col[:, None] * inv], axis=-1)
    return jnp.cos(ang), jnp.sin(ang)

def apply_rope(x, rope):
    cos, sin = rope
    xf = x.astype(jnp.float32)
    h = x.shape[-1] // 2
    x1, x2 = xf[..., :h], xf[..., h:]
    cs, sn = cos[None, :, None, :], sin[None, :, None, :]
    return jnp.concatenate([x1 * cs - x2 * sn, x1 * sn + x2 * cs], axis=-1).astype(x.dtype)

def split_in(z):
    points = np.cumsum(IN_SIZES)[:-1].tolist()
    return jnp.split(z, points, axis=-1)

def mixer_keys_values(z, kv_gain, w_ukv, ropes):
    B, L, _ = z.shape
    _, ckv, kr, _, bk, bv, _, dk, dv, _ = split_in(z)
    kva = (rms_norm(ckv, kv_gain) @ w_ukv).reshape(B, L, MLA_HEADS, MLA_NOPE + MLA_V)
    k_nope, va = kva[..., :MLA_NOPE], kva[..., MLA_NOPE:]
    k_rope = kr.reshape(B, L, 1, MLA_ROPE)
    bk = bk.reshape(B, L, SWA_KV_HEADS, SWA_HEAD_DIM)
    bv = bv.reshape(B, L, SWA_KV_HEADS, SWA_HEAD_DIM)
    dk = dk.reshape(B, L, 2 * DIFF_HEADS, DIFF_QK)
    dv = dv.reshape(B, L, DIFF_HEADS, DIFF_V)
    if ropes is not None:
        rope_a, rope_b, rope_c = ropes
        k_rope = apply_rope(k_rope, rope_a)
        bk = apply_rope(bk, rope_b)
        dk = apply_rope(dk, rope_c)
    ka = jnp.concatenate([k_nope, jnp.broadcast_to(k_rope, (B, L, MLA_HEADS, MLA_ROPE))], axis=-1)
    return (ka, va, bk, bv, dk, dv)

def mixer_queries(z, q_gain, w_uq, ropes):
    B, L, _ = z.shape
    cq, _, _, bq, _, _, dq, _, _, u = split_in(z)
    qa = (rms_norm(cq, q_gain) @ w_uq).reshape(B, L, MLA_HEADS, MLA_NOPE + MLA_ROPE)
    q_nope, q_rope = qa[..., :MLA_NOPE], qa[..., MLA_NOPE:]
    bq = bq.reshape(B, L, SWA_HEADS, SWA_HEAD_DIM)
    dq = dq.reshape(B, L, 2 * DIFF_HEADS, DIFF_QK)
    if ropes is not None:
        rope_a, rope_b, rope_c = ropes
        q_rope = apply_rope(q_rope, rope_a)
        bq = apply_rope(bq, rope_b)
        dq = apply_rope(dq, rope_c)
    qa = jnp.concatenate([q_nope, q_rope], axis=-1)
    return (qa, bq, dq, u)

def sweep_query_blocks(fn, q):
    B, L = q.shape[:2]
    nb = L // QBLOCK
    qb = jnp.moveaxis(q.reshape((B, nb, QBLOCK) + q.shape[2:]), 1, 0)
    out = lax.map(fn, qb)
    return jnp.moveaxis(out, 0, 1).reshape((B, L) + out.shape[3:])

def softmax_attend(q, k, v, scale):
    s = jnp.einsum('bqhd,bkhd->bhqk', q, k).astype(jnp.float32) * scale
    p = jax.nn.softmax(s, axis=-1)
    return jnp.einsum('bhqk,bkhd->bqhd', p.astype(v.dtype), v)

def diff_attend(q, k, v, lam):
    B, Q = q.shape[:2]
    M = k.shape[1]
    s = jnp.einsum('bqhd,bkhd->bhqk', q, k).astype(jnp.float32) * DIFF_SCALE
    p = jax.nn.softmax(s, axis=-1).reshape(B, DIFF_HEADS, 2, Q, M)
    a = p[:, :, 0] - lam * p[:, :, 1]
    return jnp.einsum('bhqk,bkhd->bqhd', a.astype(v.dtype), v)

def gqa_sink_dense(q, k, v, sink):
    B, Q, H, d = q.shape
    G = H // SWA_KV_HEADS
    qg = q.reshape(B, Q, SWA_KV_HEADS, G, d)
    s = jnp.einsum('bqkgd,bmkd->bkgqm', qg, k).astype(jnp.float32) * SWA_SCALE
    sk = jnp.broadcast_to(sink.astype(jnp.float32).reshape(1, SWA_KV_HEADS, G, 1, 1), s.shape[:-1] + (1,))
    p = jax.nn.softmax(jnp.concatenate([s, sk], axis=-1), axis=-1)[..., :-1]
    o = jnp.einsum('bkgqm,bmkd->bqkgd', p.astype(v.dtype), v)
    return o.reshape(B, Q, H, d)

def window_gqa_sink(q, k, v, kc, vc, sink):
    B, L, H, d = q.shape
    G = H // SWA_KV_HEADS
    nb = L // QBLOCK
    J = 3 * QBLOCK
    C = kc.shape[1]

    def band(a):
        ap = jnp.pad(a, ((0, 0), (QBLOCK, QBLOCK), (0, 0), (0, 0))).reshape(B, nb + 2, QBLOCK, SWA_KV_HEADS, d)
        return jnp.concatenate([ap[:, :-2], ap[:, 1:-1], ap[:, 2:]], axis=2)

    kb, vb = band(k), band(v)
    qg = q.reshape(B, nb, QBLOCK, SWA_KV_HEADS, G, d)
    s_loc = jnp.einsum('bnqkgd,bnjkd->bnkgqj', qg, kb).astype(jnp.float32) * SWA_SCALE
    qpos = jnp.arange(L).reshape(nb, QBLOCK)
    kpos = (jnp.arange(nb) * QBLOCK - QBLOCK)[:, None] + jnp.arange(J)[None, :]
    rel = kpos[:, None, :] - qpos[:, :, None]
    valid = (jnp.abs(rel) <= SWA_WINDOW) & (kpos[:, None, :] >= 0) & (kpos[:, None, :] < L)
    s_loc = jnp.where(valid[None, :, None, None], s_loc, -jnp.inf)
    s_ctx = jnp.einsum('bnqkgd,bckd->bnkgqc', qg, kc).astype(jnp.float32) * SWA_SCALE
    sk = jnp.broadcast_to(sink.astype(jnp.float32).reshape(1, 1, SWA_KV_HEADS, G, 1, 1), s_loc.shape[:-1] + (1,))
    p = jax.nn.softmax(jnp.concatenate([s_loc, s_ctx, sk], axis=-1), axis=-1)
    p_loc, p_ctx = p[..., :J], p[..., J:J + C]
    o = (jnp.einsum('bnkgqj,bnjkd->bnqkgd', p_loc.astype(v.dtype), vb)
         + jnp.einsum('bnkgqc,bckd->bnqkgd', p_ctx.astype(vc.dtype), vc))
    return o.reshape(B, L, H, d)

def multiscale_pool(u, pool_w, pool_scale):
    B, L, _ = u.shape
    ug = u.reshape(B, L, len(POOL_WINDOWS), POOL_GROUP).astype(jnp.float32)
    t = jnp.arange(L)
    diffs = []
    for gi, w in enumerate(POOL_WINDOWS):
        xg = ug[:, :, gi]
        half = w // 2
        xp = jnp.pad(xg, ((0, 0), (half, w - half), (0, 0)))
        cs = jnp.concatenate([jnp.zeros((B, 1, POOL_GROUP), jnp.float32), jnp.cumsum(xp, axis=1)], axis=1)
        win_sum = cs[:, w:w + L] - cs[:, :L]
        cnt = (jnp.minimum(t - half + w, L) - jnp.maximum(t - half, 0)).astype(jnp.float32)
        diffs.append(win_sum / cnt[None, :, None] - xg)
    dg = jnp.stack(diffs, axis=2)
    y = jnp.einsum('blgc,gcd->blgd', dg, pool_w.astype(jnp.float32)).reshape(B, L, MIX_D)
    return (y * pool_scale.astype(jnp.float32)).astype(u.dtype)

def latent_mix(qx, kvx, kvc, sink, lam, lam_init, subln_g, pool_w, pool_scale):
    qa, bq, dq, u = qx
    ka, va, bk, bv, dk, dv = kvx
    kac, vac, bkc, bvc, dkc, dvc = kvc
    B, L = u.shape[:2]
    ka_all = jnp.concatenate([ka, kac], axis=1)
    va_all = jnp.concatenate([va, vac], axis=1)
    oa = sweep_query_blocks(lambda q: softmax_attend(q, ka_all, va_all, MLA_SCALE), qa)
    ob = window_gqa_sink(bq, bk, bv, bkc, bvc, sink)
    dk_all = jnp.concatenate([dk, dkc], axis=1)
    dv_all = jnp.concatenate([dv, dvc], axis=1)
    oc = sweep_query_blocks(lambda q: diff_attend(q, dk_all, dv_all, lam), dq)
    oc = rms_norm(oc, subln_g) * (1.0 - lam_init)
    od = multiscale_pool(u, pool_w, pool_scale)
    return jnp.concatenate([oa.reshape(B, L, MIX_A), ob.reshape(B, L, MIX_B),
                            oc.reshape(B, L, MIX_C), od], axis=-1)

def context_mix(qc, kvc, sink, lam, lam_init, subln_g, pool_w, pool_scale):
    qa, bq, dq, u = qc
    kac, vac, bkc, bvc, dkc, dvc = kvc
    B, C = u.shape[:2]
    oa = softmax_attend(qa, kac, vac, MLA_SCALE)
    ob = gqa_sink_dense(bq, bkc, bvc, sink)
    oc = rms_norm(diff_attend(dq, dkc, dvc, lam), subln_g) * (1.0 - lam_init)
    od = multiscale_pool(u, pool_w, pool_scale)
    return jnp.concatenate([oa.reshape(B, C, MIX_A), ob.reshape(B, C, MIX_B),
                            oc.reshape(B, C, MIX_C), od], axis=-1)

def hier_moe(h, gw, gb, ew, eb, w_gu, w_down):
    B, L, D = h.shape
    tok = h.reshape(-1, D)
    g_logits = (tok @ gw + gb).astype(jnp.float32)
    g_prob = jax.nn.softmax(g_logits, axis=-1)
    g_sel = jnp.argmax(g_logits, axis=-1)
    p_g = jnp.take_along_axis(g_prob, g_sel[:, None], axis=-1)
    e_logits = (tok @ ew + eb).astype(jnp.float32).reshape(-1, N_EXPERT_GROUPS, EXPERTS_PER_GROUP)
    e_in = jnp.take_along_axis(e_logits, g_sel[:, None, None], axis=1)[:, 0]
    top_v, top_i = lax.top_k(e_in, TOP_K_IN_GROUP)
    w_sel = jax.nn.softmax(top_v, axis=-1) * p_g
    e_idx = g_sel[:, None] * EXPERTS_PER_GROUP + top_i
    combine = jnp.sum(jax.nn.one_hot(e_idx, N_EXPERTS, dtype=jnp.float32) * w_sel[..., None], axis=1)
    y = jnp.zeros((tok.shape[0], D), jnp.float32)
    for e in range(N_EXPERTS):
        gu = tok @ w_gu[e]
        act = jax.nn.silu(gu[:, :D_EXPERT]) * gu[:, D_EXPERT:]
        y = y + combine[:, e:e + 1] * (act @ w_down[e]).astype(jnp.float32)
    return y.reshape(B, L, D).astype(h.dtype)

def setup_inputs(seed: int = 0) -> dict:
    key = jax.random.key(seed)
    ks = jax.random.split(key, 24)
    f32 = jnp.float32

    def nrm(k, shape, scale):
        return jax.random.normal(k, shape, f32) * scale

    return {
        "x": nrm(ks[0], (BATCH, SEQ, D_MODEL), 1.0),
        "c": nrm(ks[1], (BATCH, D_MODEL), 1.0),
        "ctx": nrm(ks[2], (BATCH, CTX_LEN, D_MODEL), 1.0),
        "c_ctx": nrm(ks[3], (D_MODEL,), 1.0),
        "ada_w": nrm(ks[4], (DEPTH, D_MODEL, N_MOD * D_MODEL), 0.5 * D_MODEL ** -0.5),
        "ada_b": nrm(ks[5], (DEPTH, N_MOD * D_MODEL), 0.02),
        "norm_g": 1.0 + nrm(ks[6], (DEPTH, 4, D_MODEL), 0.05),
        "w_in": nrm(ks[7], (DEPTH, D_MODEL, D_IN), D_MODEL ** -0.5),
        "mla_q_gain": 1.0 + nrm(ks[8], (DEPTH, MLA_Q_RANK), 0.05),
        "mla_kv_gain": 1.0 + nrm(ks[9], (DEPTH, MLA_KV_RANK), 0.05),
        "mla_w_uq": nrm(ks[10], (DEPTH, MLA_Q_RANK, MLA_HEADS * (MLA_NOPE + MLA_ROPE)), MLA_Q_RANK ** -0.5),
        "mla_w_ukv": nrm(ks[11], (DEPTH, MLA_KV_RANK, MLA_HEADS * (MLA_NOPE + MLA_V)), MLA_KV_RANK ** -0.5),
        "swa_sink": nrm(ks[12], (DEPTH, SWA_HEADS), 0.5),
        "diff_lambda": nrm(ks[13], (DEPTH, 4, DIFF_QK), 0.1),
        "diff_subln": 1.0 + nrm(ks[14], (DEPTH, DIFF_V), 0.05),
        "pool_w": nrm(ks[15], (DEPTH, len(POOL_WINDOWS), POOL_GROUP, POOL_GROUP), POOL_GROUP ** -0.5),
        "pool_scale": 1.0 + nrm(ks[16], (DEPTH, MIX_D), 0.1),
        "w_out": nrm(ks[17], (DEPTH, D_MIX, D_MODEL), D_MIX ** -0.5),
        "router_gw": nrm(ks[18], (DEPTH, D_MODEL, N_EXPERT_GROUPS), D_MODEL ** -0.5),
        "router_gb": nrm(ks[19], (DEPTH, N_EXPERT_GROUPS), 0.01),
        "router_ew": nrm(ks[20], (DEPTH, D_MODEL, N_EXPERTS), D_MODEL ** -0.5),
        "router_eb": nrm(ks[21], (DEPTH, N_EXPERTS), 0.01),
        "exp_w_gu": nrm(ks[22], (DEPTH, N_EXPERTS, D_MODEL, 2 * D_EXPERT), D_MODEL ** -0.5),
        "exp_w_down": nrm(ks[23], (DEPTH, N_EXPERTS, D_EXPERT, D_MODEL), D_EXPERT ** -0.5),
    }

def reference(x, c, ctx, c_ctx, ada_w, ada_b, norm_g, w_in, mla_q_gain, mla_kv_gain, mla_w_uq, mla_w_ukv,
              swa_sink, diff_lambda, diff_subln, pool_w, pool_scale, w_out, router_gw, router_gb,
              router_ew, router_eb, exp_w_gu, exp_w_down):
    B, L, D = x.shape
    ropes = (axial_rope_table(L, MLA_ROPE), axial_rope_table(L, SWA_HEAD_DIM), axial_rope_table(L, DIFF_QK))
    silu_c = jax.nn.silu(c)
    silu_cc = jax.nn.silu(c_ctx)
    h_ctx = ctx
    for layer in range(DEPTH):
        update_ctx = layer < DEPTH - 1
        mx = jnp.split((silu_c @ ada_w[layer] + ada_b[layer])[:, None, :], N_MOD, axis=-1)
        mc = jnp.split((silu_cc @ ada_w[layer] + ada_b[layer])[None, None, :], N_MOD, axis=-1)
        lam_init = 0.8 - 0.6 * math.exp(-0.3 * layer)
        dl = diff_lambda[layer].astype(jnp.float32)
        lam = jnp.exp(jnp.sum(dl[0] * dl[1])) - jnp.exp(jnp.sum(dl[2] * dl[3])) + lam_init

        hx = modulate(rms_norm(x, norm_g[layer, 0]), mx[0], mx[1])
        hc = modulate(rms_norm(h_ctx, norm_g[layer, 0]), mc[0], mc[1])
        zx = hx @ w_in[layer]
        zc = hc @ w_in[layer]
        kvx = mixer_keys_values(zx, mla_kv_gain[layer], mla_w_ukv[layer], ropes)
        kvc = mixer_keys_values(zc, mla_kv_gain[layer], mla_w_ukv[layer], None)
        qx = mixer_queries(zx, mla_q_gain[layer], mla_w_uq[layer], ropes)
        ox = latent_mix(qx, kvx, kvc, swa_sink[layer], lam, lam_init, diff_subln[layer],
                        pool_w[layer], pool_scale[layer]) @ w_out[layer]
        x = x + mx[2] * rms_norm(ox, norm_g[layer, 1])
        if update_ctx:
            qc = mixer_queries(zc, mla_q_gain[layer], mla_w_uq[layer], None)
            oc = context_mix(qc, kvc, swa_sink[layer], lam, lam_init, diff_subln[layer],
                             pool_w[layer], pool_scale[layer]) @ w_out[layer]
            h_ctx = h_ctx + mc[2] * rms_norm(oc, norm_g[layer, 1])

        fx = hier_moe(modulate(rms_norm(x, norm_g[layer, 2]), mx[3], mx[4]), router_gw[layer], router_gb[layer],
                      router_ew[layer], router_eb[layer], exp_w_gu[layer], exp_w_down[layer])
        x = x + mx[5] * rms_norm(fx, norm_g[layer, 3])
        if update_ctx:
            fc = hier_moe(modulate(rms_norm(h_ctx, norm_g[layer, 2]), mc[3], mc[4]), router_gw[layer],
                          router_gb[layer], router_ew[layer], router_eb[layer], exp_w_gu[layer], exp_w_down[layer])
            h_ctx = h_ctx + mc[5] * rms_norm(fc, norm_g[layer, 3])
    return x


_drawn_inputs = setup_inputs


def setup_inputs(seed=0):
    import zlib

    import numpy as np

    out = dict(_drawn_inputs(seed))
    spreads = {}
    factors = {'mla_kv_gain': 8.0,
     'swa_sink': 64.0,
     'router_gb': 3.499,
     'diff_subln': 5.161,
     'router_eb': 5.585}
    for name, (base, spread) in spreads.items():
        noise = np.random.default_rng([zlib.crc32(name.encode()), seed]).standard_normal(out[name].shape)
        drawn = base * np.exp(spread * noise) if base else spread * noise
        out[name] = jnp.asarray(drawn.astype(out[name].dtype))
    for name, factor in factors.items():
        out[name] = (out[name] * factor).astype(out[name].dtype)
    return out
```

```python
import concourse.bass as bass
from concourse import mybir
from contextlib import ExitStack
import numpy as np

F32 = mybir.dt.float32
BF16 = mybir.dt.bfloat16
I32 = mybir.dt.int32
ALU = mybir.AluOpType
ACT = mybir.ActivationFunctionType
AX = mybir.AxisListType
ds = bass.ds

P = 128
D = 1024
KD = D // P
SEQ = 256
NTOK = 512
DEPTH = 2
GRID_W = 64
EPS = 1e-6
HEADS = 4
MLA_NOPE, MLA_ROPE, MLA_V = 64, 32, 64
MLA_QK = MLA_NOPE + MLA_ROPE
MLA_SCALE = MLA_QK ** -0.5
SWA_D, SWA_WINDOW = 64, 128
SWA_SCALE = SWA_D ** -0.5
DIFF_QK = 32
DIFF_SCALE = DIFF_QK ** -0.5
N_EXP, N_GRP, PER_GRP, F_EXP = 16, 4, 4, 512
BLK = 64
MAXBLK = (2 * NTOK + N_EXP * (BLK - 1)) // BLK
COLS = MAXBLK + 3
LAM_INIT = [0.8 - 0.6 * float(np.exp(-0.3 * L)) for L in range(DEPTH)]
NEG = -1e30
LN_EXP = "natural_log_exp_and_others"

C_CQ, C_CKV, C_KR, C_BQ, C_BK, C_BV, C_DQ, C_DK, C_DV, C_U, C_END = (
    0, 256, 384, 416, 672, 800, 928, 1184, 1440, 1696, 1952)
IN_CHUNKS = [(C_CQ, C_BQ), (C_BQ, C_DQ), (C_DQ, C_DV), (C_DV, C_END)]

CST = {}


def constants():
    cols, parts = 0, []

    def put(name, a):
        nonlocal cols
        full = np.zeros((P, a.shape[1]), np.float32)
        full[:a.shape[0]] = a
        CST[name] = (cols, cols + a.shape[1])
        cols += a.shape[1]
        parts.append(full)

    def rot(dim, start, stop):
        r, h = np.zeros((P, P), np.float32), dim // 2
        for b in range(start, stop, dim):
            for i in range(h):
                r[b + i + h, b + i] = -1.0
                r[b + i, b + i + h] = 1.0
        return r

    def rope(dim, start, stop):
        rows = SEQ // GRID_W
        row = np.repeat(np.arange(rows), GRID_W).astype(np.float32)
        col = np.tile(np.arange(GRID_W), rows).astype(np.float32)
        n = dim // 4
        inv = (10000.0 ** (-np.arange(n, dtype=np.float32) / n)).astype(np.float32)
        ang = np.concatenate([row[:, None] * inv, col[:, None] * inv], -1)
        c, s = np.ones((P, SEQ), np.float32), np.zeros((P, SEQ), np.float32)
        for b in range(start, stop, dim):
            for i in range(dim):
                c[b + i] = np.cos(ang[:, i % (dim // 2)])
                s[b + i] = np.sin(ang[:, i % (dim // 2)])
        return c, s

    put("ident", np.eye(P))
    for name, dim, a, b in (("mla", MLA_ROPE, MLA_NOPE, MLA_QK), ("swa", SWA_D, 0, P), ("diff", DIFF_QK, 0, P)):
        put("rot_" + name, rot(dim, a, b))
        c, s = rope(dim, a, b)
        put("cos_" + name, c)
        put("sin_" + name, s)
    t = np.arange(SEQ)
    inv_count = np.zeros((P, 2, SEQ), np.float32)
    for g, w in enumerate((2, 4, 8, 16)):
        cnt = np.minimum(t - w // 2 + w, SEQ) - np.maximum(t - w // 2, 0)
        inv_count[64 * (g % 2):64 * (g % 2) + 64, g // 2] = 1.0 / cnt
    put("inv_count", inv_count.reshape(P, -1))
    put("before", np.triu(np.ones((P, P)), 1))
    q, k = np.arange(P)[:, None], np.arange(SEQ)[None]
    put("band", np.concatenate([np.where(np.abs(k - q - P * i) <= SWA_WINDOW, 0.0, NEG) for i in range(2)], 1))
    put("more", np.tile(BLK * np.arange(1, 8) + 1, (P, 1)))
    put("count", np.tile(np.arange(BLK), (P, 1)))
    put("token", np.arange(P)[:, None] + P * np.arange(4)[None])
    put("first", np.tile(4.0 - np.arange(4), (P, 1)))
    half = (np.arange(P) // DIFF_QK) % 2
    put("parity", np.stack([1 - half, half], 1))
    put("eps", np.full((P, 1), EPS))
    return np.concatenate(parts, 1)


CONSTANTS = constants()


class Marks:

    def __init__(self, nc, ctx, known):
        self.nc, self.ctx, self.known = nc, ctx, known
        self.sems, self.count, self.where, self.bank_of, self.order = {}, {}, {}, {}, []

    def sem(self, name):
        if name not in self.sems:
            self.sems[name] = self.ctx.enter_context(self.nc.semaphore(name))
        return self.sems[name]

    def mark(self, family, *keys, by=1):
        self.count[family] = self.count.get(family, 0) + by
        for key in keys:
            assert key not in self.where, key
            self.where[key] = (family, self.count[family])
        return self.sem(family), by

    def name(self, family, key):
        self.where[key] = (family, self.count[family])

    def at(self, *key):
        if self.known is None:
            return self.sem("unknown"), 1
        family, n = self.known.where[key]
        return self.sem(family), n

    def bank(self, *job):
        return (self.known or self).bank_of.get(job, 0)

    def take(self, n_ring, *job):
        n = len(self.order)
        self.order.append(job)
        self.bank_of[job] = n % n_ring
        return n % n_ring, self.order[n - n_ring] if n >= n_ring else None


def hybrid_block(nc, A, out, known=None):
    ctx = ExitStack()
    with ctx:
        M = Marks(nc, ctx, known)
        mark, at, sem = M.mark, M.at, M.sem

        def sb(name, shape, dt=F32):
            return ctx.enter_context(nc.sbuf_tensor(name, shape, dt))

        def scratch(name, shape, dt=F32):
            return nc.dram_tensor(name, shape, dt, kind="Internal").ap()

        h_rows = [scratch(f"h_rows{L}", (NTOK if L == 0 else SEQ, D)) for L in range(DEPTH)]
        y_rows = scratch("y_rows", (BLK * (MAXBLK + 1), D))

        EXP_W = 12 * D
        W = [sb(f"weights{i}", [P, EXP_W]) for i in range(2)]
        w_gu = [W[i][:, 0:8 * D].rearrange("p (k c h n) -> p k h c n", k=KD, c=2, h=2) for i in range(2)]
        w_gu_in = [W[i][:, 0:8 * D].rearrange("p (k n) -> p k n", k=KD) for i in range(2)]
        w_dn = [W[i][:, 8 * D:12 * D].rearrange("p (k n) -> p k n", k=4) for i in range(2)]
        stages = [[W[1 - L % 2][:, i * 4 * D:(i + 1) * 4 * D] for i in range(3)] for L in range(DEPTH)]

        xT = sb("xT", [P, KD, NTOK])
        hT = sb("hT", [P, KD, NTOK])
        R1 = sb("R1", [P, 4 * D])
        rows = R1[:, :].rearrange("p (t d) -> p t d", t=4)
        oT = R1[:, :].rearrange("p (k t) -> p k t", k=KD)
        mixT = hT

        def part(region, lo, n, s=None, **kw):
            a = region[:, lo:lo + n]
            return a.rearrange(s, **kw) if s else a

        places = {}
        o = 0
        for name, n, s, kw in (("qa", 4 * NTOK, "p (h t) -> p h t", dict(h=4)), ("ka", 4 * NTOK, "p (h t) -> p h t", dict(h=4)),
                               ("bq", 2 * NTOK, "p (h t) -> p h t", dict(h=2)), ("bk", NTOK, None, {}),
                               ("dq", 4 * NTOK, "p (j v t) -> p j v t", dict(j=2, v=2)),
                               ("dk", 2 * NTOK, "p (h t) -> p h t", dict(h=2)), ("va", 4 * 256, "p (t c) -> p t c", dict(t=4)),
                               ("bv", 4 * P, "p (t c) -> p t c", dict(t=4)), ("dv", 4 * 256, "p (t c) -> p t c", dict(t=4)),
                               ("dg", 2 * NTOK, "p (j t) -> p j t", dict(j=2))):
            places[name] = [part(W[L % 2], o, n, s, **kw) for L in range(DEPTH)]
            o += n
        assert o <= EXP_W
        qas, kas, bqs, bks, dqs, dks, vas, bvs, dvs, dgs = places.values()
        prob = [part(R1, i * NTOK, NTOK) for i in range(4)]
        probT = [part(R1, (4 + i) * NTOK, NTOK, "p (k q) -> p k q", k=4) for i in range(2)]
        rope_c = [part(R1, 6 * NTOK + i * SEQ, SEQ) for i in range(2)]
        rope_s = [part(R1, 7 * NTOK + i * SEQ, SEQ) for i in range(2)]
        xg_in = [R1[0:BLK, i * D:(i + 1) * D] for i in range(2)]
        xg = R1[0:BLK, 2 * D:3 * D]
        xgT = part(R1, 3 * D, KD * BLK, "p (k s) -> p k s", k=KD)
        ya = hT[:, :, :].rearrange("p k t -> p (k t)").rearrange("p (t d) -> p t d", t=4)
        yb = rows

        lat = sb("lat", [P, 4 * NTOK])
        cq = part(lat, 0, 2 * NTOK, "p (j t) -> p j t", j=2)
        ckv = part(lat, 2 * NTOK, NTOK)
        kr = part(lat, 3 * NTOK, NTOK)
        y_sb = [part(lat, i * 512, 512) for i in range(2)]
        silu_g, act_rows = (part(lat, 1024 + i * 256, 256) for i in range(2))
        actT = part(lat, 1536, 256, "p (c s) -> p c s", c=2)
        om = [part(lat, i * 4 * 256, 4 * 256, "p (q c) -> p q c", q=4) for i in range(2)]
        PADW = 288
        up = [sb(f"up{j}", [P, 2, PADW]) for j in range(2)]
        pa = sb("pa", [P, 2, PADW])
        pb = sb("pb", [P, 2, PADW])
        sq = [sb(f"sq{i}", [P, NTOK]) for i in range(2)]
        rstd = sb("rstd", [P, NTOK])
        cst = sb("cst", [P, CONSTANTS.shape[1]])
        ones = sb("ones", [P, P])
        band = sb("band", [P, 2 * SEQ], BF16)
        ident16 = sb("ident16", [P, P], BF16)
        w_uq = sb("w_uq", [P, 2, 384])
        w_ukv = sb("w_ukv", [P, 512])
        w_rt = sb("w_rt", [P, KD, 20])
        w_pool = sb("w_pool", [P, 2, P])
        vec_rows = sb("vec_rows", [P, P])
        bias_rows = sb("bias_rows", [P, P])
        vecT = sb("vecT", [P, 74])
        ada_bT = sb("ada_bT", [P, 96])
        c_sb = sb("c_sb", [P, 2, KD])
        c_t = sb("c_t", [P, 2, KD])
        silu_c = sb("silu_c", [P, KD, 32])
        ada_sb = sb("ada_sb", [P, 512])
        mod = [sb(f"mod{L}", [P, 48, 2]) for L in range(DEPTH)]
        amp = [sb(f"amp{L}", [P, 4, KD, 2]) for L in range(DEPTH)]
        rt_b = sb("rt_b", [P, DEPTH, 20])
        neg_sink = sb("neg_sink", [P, DEPTH * 4])
        dl = sb("dl", [P, DEPTH, 4, DIFF_QK])
        dlp = sb("dlp", [P, DEPTH, 2, DIFF_QK])
        dls = sb("dls", [P, DEPTH * 2])
        neg_lam = sb("neg_lam", [P, DEPTH])
        subln = sb("subln", [P, DEPTH, 64])
        st = sb("st", [P, 8, 8])
        dstat = sb("dstat", [P, 4, 16])
        lg = sb("lg", [P, 4, 20])
        rs = sb("rs", [P, 40, 4])
        r4 = sb("r4", [P, 10, 4, 4])
        r16 = sb("r16", [P, 6, 4, 16])
        cmp7 = sb("cmp7", [P, 16, 7])
        e16 = sb("e16", [P, 5, 16])
        spos = sb("spos", [P, 2, 4], I32)
        spos_t = sb("spos_t", [P, 2, 2, 4], I32)
        spos_f = sb("spos_f", [P, 2, 2, 4])
        chosen = sb("chosen", [P, 5, 16])
        place_hot = part(lat, 0, 8 * BLK, "p (i s) -> p i s", i=8)
        block_id = part(lat, 8 * BLK, 8 * COLS, "p (i b) -> p i b", i=8)
        lgT = part(lat, 2 * NTOK, NTOK)
        zeros = sb("zeros", [P, D // 2])
        slots = sb("slots", [BLK, COLS], I32)
        slot_col = sb("slot_col", [BLK, 2], I32)
        tabs = [sb(f"tab{L}", [P, 64], I32) for L in range(DEPTH)]
        T_NB, T_START, T_CUM, T_TOTAL = 0, 16, 32, 48

        psum = ctx.enter_context(nc.psum_tensor("psum", [P, 8, 512], F32))
        RING, B_SUM, B_ADA = 6, 6, 7

        def C(name, rows_=P):
            a, b = CST[name]
            return cst[0:rows_, a:b]

        ident = C("ident")
        inv_count = C("inv_count").rearrange("p (j t) -> p j t", j=2)

        def gain(L, i, k):
            return vecT[:, L * 32 + i * 8 + k:L * 32 + i * 8 + k + 1]

        def q_tokens(L):
            return NTOK if L == 0 else SEQ

        def streams(n):
            return [(s, s * SEQ, (s + 1) * SEQ) for s in range(n // SEQ)]

        KINDS = ("mla", "swa", "diff")

        def units(L):
            return [(kind, qt, h) for kind in KINDS for qt in range(q_tokens(L) // P) for h in range(HEADS)]

        TILES = {"cq0": (0, 0), "cq1": (P, 0), "ckv": (C_CKV, 1), "kr": (C_KR, 1), "bk": (C_BK - C_BQ, 1), "bq0": (0, 0),
                 "bq1": (0, 0), "dq0": (0, 0), "dq1": (P, 0), "dk0": (C_DK - C_DQ, 1), "dk1": (C_DK - C_DQ + P, 1),
                 "u0": (C_U - C_DV, 0), "u1": (C_U - C_DV + P, 0)}
        VALUES = {"bv": (P, range(4)), "dv0": (256, range(2)), "dv1": (256, range(2, 4))}
        ROPES = [{"kr": (kr[64:96, 0:SEQ], "mla", 64, 96), "bk": (bks[L][:, 0:SEQ], "swa", 0, P)} for L in range(DEPTH)]
        for L in range(DEPTH):
            for j in range(2):
                ROPES[L][f"bq{j}"] = (bqs[L][:, j, 0:SEQ], "swa", 0, P)
                ROPES[L][f"dq{j}"] = (dqs[L][:, j, 0, 0:SEQ], "diff", 0, P)
                ROPES[L][f"dk{j}"] = (dks[L][:, j, 0:SEQ], "diff", 0, P)
            for i in range(HEADS):
                ROPES[L][f"qa{i}"] = (qas[L][0:MLA_QK, i, 0:SEQ], "mla", 0, MLA_QK)

        items = []
        for i in range(4):
            items.append(("ada", 0, i))
        for i in range(4):
            items.append(("in", 0, i))
        items += [("ada", 0, i) for i in range(4, 12)] + [("ada", 1, i) for i in range(12)]
        items += [("out", 0, i) for i in range(2)]
        n_stage0 = len(items)
        items += [("in", 1, i) for i in range(4)] + [("out", 1, i) for i in range(2)]
        item_no = {it: n for n, it in enumerate(items)}

        def stage_source(it):
            kind, L, i = it
            if kind == "ada":
                r, kk = i // 4, i % 4
                return A["ada_w"][L].rearrange("(p k) n -> p k n", k=KD)[:, 2 * kk:2 * kk + 2, r * 2048:(r + 1) * 2048]
            if kind == "in":
                a, b = IN_CHUNKS[i]
                return A["w_in"][L].rearrange("(k p) n -> p k n", p=P)[:, :, a:b]
            return A["w_out"][L].rearrange("(k p) n -> p k n", p=P)[:, :, i * 512:(i + 1) * 512]

        def stage_buffer(n):
            return stages[0][n % 3] if n < n_stage0 else stages[1][(n - n_stage0) % 3]

        def staged(it):
            kind, L, i = it
            b = stage_buffer(item_no[it])
            if kind == "ada":
                return b.rearrange("p (k g n) -> p k g n", k=2, g=4)
            n = IN_CHUNKS[i][1] - IN_CHUNKS[i][0] if kind == "in" else 512
            return b[:, 0:KD * n].rearrange("p (k n) -> p k n", k=KD)

        def ada_plan(L):
            return [it for it in items if it[0] == "ada" and item_no[it] >= 8] if L == 0 else []

        block = ctx.enter_context(nc.Block())

        @block.tensor
        def _(pe):
            def take(*job):
                b, before = M.take(RING, *job)
                if before is not None:
                    pe.wait_ge(*at("read", *before))
                return psum[:, b, :]

            sums = []

            def square_sum(S, tag, n, count, buf):
                for k in range(count):
                    square_part(S, tag, n, k, count, buf(k))

            def square_part(S, tag, n, k, count, src):
                if k == 0:
                    if sums:
                        pe.wait_ge(*at("sum_read", sums[-1]))
                    sums.append(tag)
                pe.wait_ge(*at("sq", tag, k))
                nc.tensor.matmul(psum[:, B_SUM, 0:n], ones[:, :], src, start=(k == 0), stop=(k == count - 1))\
                    .then_inc(*mark(S, ("sq_used", tag, k)))

            def ada_item(S, it):
                _, L, i = it
                pe.wait_ge(*at("staged", item_no[it]))
                r, kk = i // 4, i % 4
                if kk == 0 and (L, r) != (0, 0):
                    pe.wait_ge(*at("ada_sb", *((L, r - 1) if r else (L - 1, 2))))
                w = staged(it)
                for k2 in range(2):
                    k = 2 * kk + k2
                    for g in range(4):
                        mm = nc.tensor.matmul(psum[32 * g:32 * g + 32, B_ADA, :], silu_c[:, k, :], w[:, k2, g, :],
                                              start=(k == 0), stop=(k == 7), skip_group_check=True)
                mm.then_inc(*mark(S, ("used", item_no[it])))

            def ada_turn(S, L, r):
                pe.wait_ge(*at("ada_sb", L, r))
                t = take("adaT", L, r)
                for q in range(4):
                    mm = nc.tensor.transpose(t[:, q * P:(q + 1) * P], ada_sb[:, q * P:(q + 1) * P], ident)
                mm.then_inc(*mark(S, ("filled", "adaT", L, r)))

            def norm(L, w, n):
                square_sum(f"pe_norm{w}{L}", (L, w), n, KD, lambda k: sq[k % 2][:, 0:n])

            def project(L):
                S, nq = f"pe_in{L}", q_tokens(L)
                pe.wait_ge(*at("h", L, 1, KD - 1))
                for c, names in enumerate((("cq0", "cq1", "ckv", "kr"), ("bk", "bv", "bq0", "bq1"),
                                           ("dq0", "dk0", "dq1", "dk1"), ("dv0", "dv1", "u0", "u1"))):
                    it = ("in", L, c)
                    pe.wait_ge(*at("staged", item_no[it]))
                    w = staged(it)
                    for name in names:
                        t = take(name, L)
                        if name in VALUES:
                            width, tts = VALUES[name]
                            col = (C_BV - C_BQ) if name == "bv" else 0
                            for i, tt in enumerate(tts):
                                for k in range(KD):
                                    mm = nc.tensor.matmul(t[:, i * width:(i + 1) * width], hT[:, k, tt * P:(tt + 1) * P],
                                                          w[:, k, col:col + width], start=(k == 0), stop=(k == KD - 1))
                        else:
                            col, n = TILES[name]
                            n = NTOK if n else nq
                            m, lo = (MLA_ROPE, MLA_NOPE) if name == "kr" else (P, 0)
                            for k in range(KD):
                                if name in ("bq0", "bq1"):
                                    for b in range(2):
                                        c0 = b * P + int(name[2]) * 64
                                        mm = nc.tensor.matmul(t[64 * b:64 * b + 64, 0:n], w[:, k, c0:c0 + 64], hT[:, k, 0:n],
                                                              start=(k == 0), stop=(k == KD - 1), skip_group_check=True)
                                else:
                                    mm = nc.tensor.matmul(t[lo:lo + m, 0:n], w[:, k, col:col + m], hT[:, k, 0:n],
                                                          start=(k == 0), stop=(k == KD - 1))
                        used = [("used", item_no[it])] if name == names[-1] else []
                        mm.then_inc(*mark(S, ("filled", name, L), *used))
                        if name == "bk":
                            square_sum(S, ("cq", L), nq, 2, lambda j: sq[j][:, 0:nq])
                        if name == "bq1":
                            square_sum(S, ("ckv", L), NTOK, 1, lambda j: sq[0][:, :])

            def rotate(S, L, name, x, kind, lo, hi):
                pe.wait_ge(*at("tile", L, name))
                t = take("rot", L, name)
                r = C("rot_" + kind)
                nc.tensor.matmul(t[lo:hi, 0:SEQ], r[lo:hi, lo:hi], x, start=True, stop=True)\
                    .then_inc(*mark(S, ("filled", "rot", L, name)))

            def latent_projections(L):
                S, nq = f"pe_lat{L}", q_tokens(L)
                for name in ("kr", "bk", "bq0", "bq1"):
                    x, kind, lo, hi = ROPES[L][name]
                    rotate(S, L, name, x, kind, lo, hi)
                pe.wait_ge(*at("small_w", L))
                pe.wait_ge(*at("cqn", L))
                for h in range(HEADS):
                    t = take("qa", L, h)
                    for j in range(2):
                        mm = nc.tensor.matmul(t[0:MLA_QK, 0:nq], w_uq[:, j, h * MLA_QK:(h + 1) * MLA_QK], cq[:, j, 0:nq],
                                              start=(j == 0), stop=(j == 1))
                    mm.then_inc(*mark(S, ("filled", "qa", L, h)))
                pe.wait_ge(*at("ckvn", L))
                for h in range(HEADS):
                    t = take("ka", L, h)
                    nc.tensor.matmul(t[0:MLA_NOPE, :], w_ukv[:, h * P:h * P + MLA_NOPE], ckv, start=True, stop=True)\
                        .then_inc(*mark(S, ("filled", "ka", L, h)))
                wv = w_ukv[:, :].rearrange("p (h c) -> p h c", h=HEADS)[:, :, MLA_NOPE:P]
                for j in range(2):
                    t = take("va", L, j)
                    for i in range(2):
                        tt = 2 * j + i
                        mm = nc.tensor.matmul(t[:, i * 256:(i + 1) * 256], ckv[:, tt * P:(tt + 1) * P], wv,
                                              start=True, stop=True)
                    mm.then_inc(*mark(S, ("filled", "va", L, j)))
                for name in ("qa0", "qa1", "qa2", "qa3", "dq0", "dk0", "dq1", "dk1"):
                    x, kind, lo, hi = ROPES[L][name]
                    rotate(S, L, name, x, kind, lo, hi)

            def mix(L):
                S = f"pe_mix{L}"
                U, nq = units(L), q_tokens(L)
                ada, done = ada_plan(L), 0

                def scores(u):
                    kind, qt, h = U[u]
                    nk = NTOK if qt < 2 else SEQ
                    keys, qs = slice(NTOK - nk, NTOK), slice(qt * P, (qt + 1) * P)
                    if kind == "mla":
                        if qt == 0:
                            pe.wait_ge(*at("roped", L, f"qa{h}"))
                            pe.wait_ge(*at("ka", L, h))
                            pe.wait_ge(*at("kr_out", L, h))
                        t = take("s", L, u, 0)
                        nc.tensor.matmul(t[:, 0:nk], qas[L][0:MLA_QK, h, qs], kas[L][0:MLA_QK, h, keys], start=True, stop=True)\
                            .then_inc(*mark(S, ("filled", "s", L, u, 0)))
                    elif kind == "swa":
                        if qt == 0 and h == 0:
                            pe.wait_ge(*at("roped", L, "bq1"))
                        t = take("s", L, u, 0)
                        lo, local = 64 * (h // 2), qt < 2
                        if local:
                            nc.tensor.matmul(t[:, 0:SEQ], bqs[L][lo:lo + 64, h % 2, qs], bks[L][lo:lo + 64, 0:SEQ], start=True, stop=False)
                            nc.tensor.matmul(t[:, 0:SEQ], ident16[:, :], band[:, qt * SEQ:(qt + 1) * SEQ], start=False, stop=True)
                        mm = nc.tensor.matmul(t[:, nk - SEQ:nk], bqs[L][lo:lo + 64, h % 2, qs], bks[L][lo:lo + 64, SEQ:NTOK],
                                              start=True, stop=True)
                        mm.then_inc(*mark(S, ("filled", "s", L, u, 0)))
                    else:
                        if qt == 0 and h == 0:
                            pe.wait_ge(*at("dq_split", L, 1))
                            pe.wait_ge(*at("roped", L, "dk1"))
                        j, lo = h // 2, 64 * (h % 2)
                        for v in range(2):
                            t = take("s", L, u, v)
                            nc.tensor.matmul(t[:, 0:nk], dqs[L][lo:lo + 64, j, v, qs], dks[L][lo:lo + 64, j, keys],
                                             start=True, stop=True).then_inc(*mark(S, ("filled", "s", L, u, v)))

                def turn(u):
                    kind, qt, h = U[u]
                    pe.wait_ge(*at("prob", L, u))
                    t = take("pT", L, u)
                    for i in range(4 if qt < 2 else 2):
                        mm = nc.tensor.transpose(t[:, i * P:(i + 1) * P], prob[u % 3][:, i * P:(i + 1) * P], ident)
                    mm.then_inc(*mark(S, ("filled", "pT", L, u)))

                def values(u):
                    kind, qt, h = U[u]
                    n, k0 = (4, 0) if qt < 2 else (2, 2)
                    pe.wait_ge(*at("probT", L, u))
                    if qt == 0 and h == 0:
                        pe.wait_ge(*at("v", L, kind))
                    t = take("o", L, u)
                    for i in range(n):
                        v = {"mla": vas[L][:, k0 + i, h * 64:h * 64 + 64], "diff": dvs[L][:, k0 + i, h * 64:h * 64 + 64],
                             "swa": bvs[L][:, k0 + i, (h // 2) * 64:(h // 2) * 64 + 64]}[kind]
                        mm = nc.tensor.matmul(t[:, 0:64], probT[u % 2][:, i, :], v, start=(i == 0), stop=(i == n - 1))
                    mm.then_inc(*mark(S, ("filled", "o", L, u)))

                def merge(kind):
                    pe.wait_ge(*at("om", L, kind))
                    for j in range(2):
                        t = take("mT", L, kind, j)
                        for qt in range(nq // P):
                            mm = nc.tensor.transpose(t[:, qt * P:(qt + 1) * P],
                                                     om[KINDS.index(kind) % 2][:, qt, j * P:(j + 1) * P], ident)
                        mm.then_inc(*mark(S, ("filled", "mT", L, kind, j)))

                per = len(U) // 3
                for i in range(len(U) + 3):
                    if i < len(U):
                        scores(i)
                    if 2 <= i < len(U) + 2:
                        turn(i - 2)
                    if i >= 3:
                        values(i - 3)
                    if i in (per + 7, 2 * per + 7):
                        merge(KINDS[(i - 7) // per - 1])
                    while done < len(ada) and done * len(U) <= i * len(ada):
                        ada_item(S, ada[done])
                        _, la, ia = ada[done]
                        done += 1
                        if ia % 4 == 1 and (la, ia) != (0, 5):
                            ada_turn(S, *((la, ia // 4 - 1) if ia // 4 else (la - 1, 2)))
                if ada:
                    ada_turn(S, 1, 2)
                for j in range(2):
                    pe.wait_ge(*at("dg", L, j))
                    t = take("pool", L, j)
                    nc.tensor.matmul(t[:, 0:nq], w_pool[:, j, :], dgs[L][:, j, 0:nq], start=True, stop=True)\
                        .then_inc(*mark(S, ("filled", "pool", L, j)))
                merge("diff")

            def project_out(L):
                S, nq = f"pe_out{L}", q_tokens(L)
                pe.wait_ge(*at("mixT", L))
                for m in range(KD):
                    it = ("out", L, m // 4)
                    if m % 4 == 0:
                        pe.wait_ge(*at("staged", item_no[it]))
                    w = staged(it)
                    t = take("oT", L, m)
                    for k in range(KD):
                        mm = nc.tensor.matmul(t[:, 0:nq], w[:, k, (m % 4) * P:(m % 4 + 1) * P], mixT[:, k, 0:nq],
                                              start=(k == 0), stop=(k == KD - 1))
                    used = [("used", item_no[it])] if m % 4 == 3 else []
                    mm.then_inc(*mark(S, ("filled", "oT", L, m), *used))
                    if m:
                        square_part(S, ("o", L), nq, m - 1, KD, sq[(m - 1) % 2][:, 0:nq])
                square_part(S, ("o", L), nq, KD - 1, KD, sq[(KD - 1) % 2][:, 0:nq])

            def route(L):
                S, nt = f"pe_route{L}", q_tokens(L) // P
                pe.wait_ge(*at("h", L, 2, KD - 1))
                pe.wait_ge(*at("small_w", L))
                t = take("lgT", L)
                for k in range(KD):
                    mm = nc.tensor.matmul(t[0:20, 0:nt * P], w_rt[:, k, :], hT[:, k, 0:nt * P], start=(k == 0), stop=(k == KD - 1))
                mm.then_inc(*mark(S, ("filled", "lgT", L)))
                pe.wait_ge(*at("lgT", L))
                t = take("lg", L)
                for tt in range(nt):
                    mm = nc.tensor.transpose(t[:, tt * 20:tt * 20 + 20], lgT[0:20, tt * P:(tt + 1) * P], ident[0:20, 0:20])
                mm.then_inc(*mark(S, ("filled", "lg", L)))
                for tt in range(nt):
                    for half in range(2):
                        t = take("hr", L, tt, half)
                        for i in range(4):
                            mm = nc.tensor.transpose(t[:, i * P:(i + 1) * P], hT[:, 4 * half + i, tt * P:(tt + 1) * P], ident)
                        mm.then_inc(*mark(S, ("filled", "hr", L, tt, half)))
                pe.wait_ge(*at("chosen", L))
                t = take("rk", L)
                nc.tensor.matmul(t[:, 0:(nt + 1) * 16], C("before"), chosen[:, 4 - nt:5, :], start=True, stop=False)
                for i in range(nt):
                    mm = nc.tensor.matmul(t[:, (i + 1) * 16:(nt + 1) * 16], ones[:, :],
                                          chosen[:, 4 - nt + i, :].unsqueeze(1).to_broadcast([P, nt - i, 16]),
                                          start=False, stop=(i == nt - 1))
                mm.then_inc(*mark(S, ("filled", "rk", L)))
                pe.wait_ge(*at("slot_hot", L))
                t = take("st", L)
                for i in range(2 * nt):
                    mm = nc.tensor.matmul(t[0:BLK, 0:COLS], place_hot[:, i, :], block_id[:, i, :], start=(i == 0), stop=(i == 2 * nt - 1))
                mm.then_inc(*mark(S, ("filled", "st", L)))

            def experts(L):
                for job in M.order[-RING:]:
                    pe.wait_ge(*at("read", *job))
                xt_ps, gu_ps, at_ps, y_ps = (psum[:, b, :] for b in range(4))
                x_rows, x_turned, x_ready = sem(f"x_rows{L}"), sem(f"x_turned{L}"), sem(f"x_ready{L}")
                gu_done, act_ready = sem(f"gu_done{L}"), sem(f"act_ready{L}")
                act_turned, actT_ready, y_done = sem(f"act_turned{L}"), sem(f"actT_ready{L}"), sem(f"y_done{L}")

                def turn_x(g):
                    pe.wait_ge(x_rows, g + 1)
                    pe.sem_inc(sem("pe_hold"), 1)
                    for k in range(KD):
                        mm = nc.tensor.transpose(xt_ps[:, k * BLK:(k + 1) * BLK], xg[:, k * P:(k + 1) * P], ident[0:BLK, 0:BLK])
                    mm.then_inc(x_turned, 1)

                def gate_up(g, place):
                    pe.wait_ge(x_ready, g + 1)
                    for k in range(KD):
                        for j in range(2):
                            mm = nc.tensor.matmul(gu_ps[64 * j:64 * j + 64, :], xgT[:, k, :], w_gu[place][:, k, j, :, :],
                                                  start=(k == 0), stop=(k == KD - 1), skip_group_check=True)
                    mm.then_inc(gu_done, 1)

                def turn_act(g):
                    pe.wait_ge(act_ready, g + 1)
                    for c in range(2):
                        mm = nc.tensor.transpose(at_ps[:, c * P:(c + 1) * P], act_rows[:, c * P:(c + 1) * P], ident)
                    mm.then_inc(act_turned, 1)

                def down(g, place):
                    pe.wait_ge(actT_ready, g + 1)
                    for kk in range(4):
                        for j in range(2):
                            mm = nc.tensor.matmul(y_ps[64 * j:64 * j + 64, :],
                                                  actT[:, kk % 2, (kk // 2) * 64:(kk // 2) * 64 + 64],
                                                  w_dn[place][:, kk, j * 512:(j + 1) * 512],
                                                  start=(kk == 0), stop=(kk == 3), skip_group_check=True)
                    mm.then_inc(y_done, 1)

                turn_x(0)
                pe.wait_ge(*at("tab", L))
                with pe.Fori(0, N_EXP // 2) as pair:
                    for par in range(2):
                        place = (par + L) % 2
                        n_blocks = pe.value_load(tabs[L][0:1, ds(pair * 2 + (T_NB + par), 1)], min_val=1, max_val=8)
                        start = pe.value_load(tabs[L][0:1, ds(pair * 2 + (T_START + par), 1)], min_val=0, max_val=MAXBLK)
                        pe.wait_ge(sem(f"w_gu{place}"), (pair + (L * (N_EXP // 2) + 1)) * 32)
                        pe.sem_inc(sem("pe_hold"), 1)
                        gate_up(start, place)
                        turn_x(start + 1)
                        if par:
                            down(start - 1, 1 - place)
                        else:
                            with pe.If(pair > 0):
                                down(start - 1, 1 - place)
                        turn_act(start)
                        pe.wait_ge(sem(f"w_dn{place}"), (pair + (L * (N_EXP // 2) + 1)) * 16)
                        pe.sem_inc(sem("pe_hold"), 1)
                        with pe.If(n_blocks > 1):
                            with pe.Fori(start + 1, start + n_blocks) as g:
                                gate_up(g, place)
                                turn_x(g + 1)
                                down(g - 1, place)
                                turn_act(g)
                total = pe.value_load(tabs[L][0:1, T_TOTAL:T_TOTAL + 1], min_val=N_EXP, max_val=MAXBLK)
                down(total - 1, 1 - L % 2)
                pe.wait_ge(y_done, total)
                pe.wait_ge(x_ready, total + 1)
                for s in (gu_done, x_turned, act_turned, y_done):
                    pe.sem_inc(s, 1)

            def combine(L):
                S, nt = f"pe_comb{L}", q_tokens(L) // P
                pe.wait_ge(*at("banks_out", L))
                pe.wait_ge(*at("y_norm", L, nt - 1))
                for k in range(KD):
                    t = take("yT", L, k)
                    for tt in range(nt):
                        mm = nc.tensor.transpose(t[:, tt * P:(tt + 1) * P], ya[:, tt, k * P:(k + 1) * P], ident)
                    mm.then_inc(*mark(S, ("filled", "yT", L, k)))

            S0 = "pe_start"
            for key in (("const",), ("ones",), ("vec_rows",)):
                pe.wait_ge(*at(*key))
            t = take("vec")
            nc.tensor.transpose(t[:, 0:74], vec_rows[0:74, :], ident[0:74, 0:74])
            nc.tensor.transpose(t[:, P:P + 96], bias_rows[0:96, :], ident[0:96, 0:96])\
                .then_inc(*mark(S0, ("filled", "vec")))
            pe.wait_ge(*at("x_rows"))
            for k in range(KD):
                t = take("x0", k)
                for tt in range(4):
                    mm = nc.tensor.transpose(t[:, tt * P:(tt + 1) * P], rows[:, tt, k * P:(k + 1) * P], ident)
                mm.then_inc(*mark(S0, ("filled", "x0", k)))
            pe.wait_ge(*at("silu_c"))
            for i in range(4):
                ada_item(S0, ("ada", 0, i))
            norm(0, 1, NTOK)
            ada_turn(S0 + "_turn", 0, 0)
            for L in range(DEPTH):
                if L:
                    norm(L, 1, NTOK)
                project(L)
                latent_projections(L)
                mix(L)
                project_out(L)
                norm(L, 2, q_tokens(L))
                route(L)
                experts(L)
                combine(L)
            pe.wait_ge(*at("x", 1, 2, KD - 1))
            for tt in range(2):
                for half in range(2):
                    t = take("fin", tt, half)
                    for i in range(4):
                        mm = nc.tensor.transpose(t[:, i * P:(i + 1) * P], xT[:, 4 * half + i, tt * P:(tt + 1) * P], ident)
                    mm.then_inc(*mark("pe_fin", ("filled", "fin", tt, half)))

        def read(eng, *job):
            eng.wait_ge(*at("filled", *job))
            return psum[:, M.bank(*job), :]

        @block.scalar
        def _(act):
            a = nc.scalar.activation
            squared = {}

            def square(S, tag, k, src, n, buf):
                if buf in squared:
                    act.wait_ge(*at("sq_used", *squared[buf]))
                squared[buf] = (tag, k)
                a(sq[buf][:, 0:n], src, ACT.Square).then_inc(*mark(S, ("sq", tag, k)))

            def finish_rstd(S, tag, last, n, width, free):
                act.wait_ge(*at("sq_used", tag, last))
                if free:
                    act.wait_ge(*at(*free))
                a(rstd[:, 0:n], psum[:, B_SUM, 0:n], ACT.Ln, scale=1.0 / width, bias=C("eps"))\
                    .then_inc(*mark(S, ("sum_read", tag)))
                act.wait_ge(*at("sum_read", tag))
                a(rstd[:, 0:n], rstd[:, 0:n], ACT.Exp, scale=-0.5).then_inc(*mark(S, ("rstd", tag)))

            def norm(L, w, n, free):
                S = f"act_norm{w}{L}"
                for k in range(KD):
                    if L == 0 and w == 1:
                        act.wait_ge(*at("read", "x0", k))
                    elif w == 1:
                        act.wait_ge(*at("x", L - 1, 2, k))
                    else:
                        act.wait_ge(*at("x", L, 1, k))
                    square(S, (L, w), k, xT[:, k, 0:n], n, k % 2)
                finish_rstd(S, (L, w), KD - 1, n, D, free)
                act.wait_ge(*at("amp", L, 0 if w == 1 else 2))
                b0 = 0 if w == 1 else 24
                for k in range(KD):
                    act.wait_ge(*at("xn", L, w, k))
                    for s, lo, hi in streams(n):
                        ins = a(hT[:, k, lo:hi], hT[:, k, lo:hi], ACT.Identity,
                                scale=amp[L][:, 0 if w == 1 else 2, k, s:s + 1], bias=mod[L][:, b0 + k, s:s + 1])
                    ins.then_inc(*mark(S, ("h", L, w, k)))

            def copy(S, dst, job, n=NTOK, lo=0, hi=P, scale=1.0, keys=()):
                src = read(act, *job)[lo:hi, 0:n]
                a(dst, src, ACT.Copy, scale=scale).then_inc(*mark(S, ("read", *job), *keys))

            def project(L):
                S, nq = f"act_in{L}", q_tokens(L)
                for j in range(2):
                    copy(S, cq[:, j, 0:nq], (f"cq{j}", L), nq)
                for j in range(2):
                    act.wait_ge(*at("read", f"cq{j}", L))
                    square(S, ("cq", L), j, cq[:, j, 0:nq], nq, j)
                copy(S, ckv, ("ckv", L))
                copy(S, kr[64:96, :], ("kr", L), lo=64, hi=96, keys=[("tile", L, "kr")])
                copy(S, bks[L], ("bk", L), keys=[("tile", L, "bk")])
                finish_rstd(S, ("cq", L), 1, nq, 256, ("xn", L, 1, KD - 1))
                square(S, ("ckv", L), 0, ckv, NTOK, 0)
                copy(S, bvs[L][:, :, :].rearrange("p t c -> p (t c)"), ("bv", L), keys=[("v", L, "swa")])
                for j in range(2):
                    copy(S, bqs[L][:, j, 0:nq], (f"bq{j}", L), nq, scale=SWA_SCALE, keys=[("tile", L, f"bq{j}")])
                finish_rstd(S, ("ckv", L), 0, NTOK, 128, ("cqn", L))
                for j in range(2):
                    copy(S, dqs[L][:, j, 0, 0:nq], (f"dq{j}", L), nq, scale=DIFF_SCALE, keys=[("tile", L, f"dq{j}")])
                    copy(S, dks[L][:, j, :], (f"dk{j}", L), keys=[("tile", L, f"dk{j}")])
                for j in range(2):
                    copy(S, dvs[L][:, 2 * j:2 * j + 2, :].rearrange("p t c -> p (t c)"), (f"dv{j}", L),
                         keys=[("v", L, "diff")] if j else [])
                for j in range(2):
                    if L == 0:
                        act.wait_ge(*at("pads"))
                    else:
                        act.wait_ge(*at("dg", L - 1, j))
                    src = read(act, f"u{j}", L)
                    ns = nq // SEQ
                    a(up[j][:, 0:ns, 16:16 + SEQ], src[:, 0:nq].rearrange("p (s t) -> p s t", s=ns), ACT.Copy)\
                        .then_inc(*mark(S, ("read", f"u{j}", L)))

            def latent_projections(L):
                S, nq = f"act_lat{L}", q_tokens(L)
                for h in range(HEADS):
                    copy(S, qas[L][0:MLA_QK, h, 0:nq], ("qa", L, h), nq, hi=MLA_QK, scale=MLA_SCALE, keys=[("tile", L, f"qa{h}")])
                for h in range(HEADS):
                    copy(S, kas[L][0:MLA_NOPE, h, :], ("ka", L, h), hi=MLA_NOPE, keys=[("ka", L, h)])
                for j in range(2):
                    copy(S, vas[L][:, 2 * j:2 * j + 2, :].rearrange("p t c -> p (t c)"), ("va", L, j),
                         keys=[("v", L, "mla")] if j else [])

            def mix(L):
                S = f"act_mix{L}"
                U, nq = units(L), q_tokens(L)
                per = len(U) // 3

                def softmax(u):
                    kind, qt, h = U[u]
                    nk = NTOK if qt < 2 else SEQ
                    act.wait_ge(*at("nmax", L, u))
                    if u >= 3:
                        act.wait_ge(*at("filled", "pT", L, u - 3))
                    if u < 3:
                        act.wait_ge(*at("roped", L, "dk1"))
                    if u >= 8:
                        act.wait_ge(*at("read", "o", L, u - 8))
                    s_ = st[:, u % 8, :]
                    for v in range(2 if kind == "diff" else 1):
                        if v == 1 and U[u - 1][0] == "diff":
                            act.wait_ge(*at("prob", L, u - 1))
                        a((prob[u % 3] if v == 0 else prob[3])[:, 0:nk], read(act, "s", L, u, v)[:, 0:nk], ACT.Exp,
                          bias=s_[:, v:v + 1], accum_out=s_[:, 2 + v:3 + v])\
                            .then_inc(*mark(S, ("read", "s", L, u, v), *([("prob", L, u)] if kind != "diff" else [])))
                    if kind == "swa":
                        a(s_[:, 4:5], neg_sink[:, L * 4 + h:L * 4 + h + 1], ACT.Exp, scale=-1.0, bias=s_[:, 0:1])\
                            .then_inc(*mark(S, ("sink", L, u)))

                def probs_out(u):
                    kind, qt, h = U[u]
                    n = 4 if qt < 2 else 2
                    src = read(act, "pT", L, u)
                    if u >= 2:
                        act.wait_ge(*at("filled", "o", L, u - 2))
                    a(probT[u % 2][:, 0:n, :], src[:, 0:n * P].rearrange("p (k q) -> p k q", k=n), ACT.Copy)\
                        .then_inc(*mark(S, ("read", "pT", L, u), ("probT", L, u)))

                def merge(kind):
                    for j in range(2):
                        copy(S, mixT[:, 2 * KINDS.index(kind) + j, 0:nq], ("mT", L, kind, j), nq,
                             keys=[("mixT", L)] if kind == "diff" and j else [])

                for i in range(len(U) + 2):
                    if i < len(U):
                        softmax(i)
                    if i >= 2:
                        probs_out(i - 2)
                    if i in (per + 8, 2 * per + 8):
                        merge(KINDS[(i - 8) // per - 1])
                for j in range(2):
                    src = read(act, "pool", L, j)
                    a(mixT[:, 6 + j, 0:nq], src[:, 0:nq], ACT.Copy, scale=vecT[:, 70 + 2 * L + j:71 + 2 * L + j])\
                        .then_inc(*mark(S, ("read", "pool", L, j)))
                act.wait_ge(*at("dsum", L))
                q = nq // P
                a(dstat[:, 0:q, 4:8], dstat[:, 0:q, 0:4], ACT.Ln, scale=1.0 / 64, bias=C("eps")).then_inc(*mark(S, ("dln", L)))
                act.wait_ge(*at("dln", L))
                a(dstat[:, 0:q, 8:12], dstat[:, 0:q, 4:8], ACT.Exp, scale=-0.5).then_inc(*mark(S, ("drstd", L)))
                merge("diff")

            def project_out(L):
                S, nq = f"act_out{L}", q_tokens(L)
                act.wait_ge(*at("amp", L, 1))
                for m in range(KD):
                    src = read(act, "oT", L, m)
                    square(S, ("o", L), m, src[:, 0:nq], nq, m % 2)
                    for s, lo, hi in streams(nq):
                        ins = a(oT[:, m, lo:hi], src[:, lo:hi], ACT.Copy, scale=amp[L][:, 1, m, s:s + 1])
                    ins.then_inc(*mark(S, ("read", "oT", L, m)))
                finish_rstd(S, ("o", L), KD - 1, nq, D, ("ckvn", L))

            def route(L):
                S, nt = f"act_route{L}", q_tokens(L) // P
                copy(S, lgT[0:20, 0:nt * P], ("lgT", L), nt * P, hi=20, keys=[("lgT", L)])
                for tt in range(nt):
                    for half in range(2):
                        copy(S, rows[:, tt, half * 512:half * 512 + 512], ("hr", L, tt, half),
                             keys=[("h_tile", L, tt)] if half else [])
                act.wait_ge(*at("g_shift", L))
                a(r4[:, 1, 0:nt, :], r4[:, 0, 0:nt, :], ACT.Exp).then_inc(*mark(S, ("g_exp", L)))
                act.wait_ge(*at("top_diff", L))
                a(rs[:, 7, 0:nt], rs[:, 6, 0:nt], ACT.Exp).then_inc(*mark(S, ("top_exp", L)))

            def experts(L):
                gu_done, silu_ready = sem(f"gu_done{L}"), sem(f"silu_ready{L}")
                act_turned, actT_ready, y_done = sem(f"act_turned{L}"), sem(f"actT_ready{L}"), sem(f"y_done{L}")
                y_copied = sem(f"y_copied{L}")

                def silu(g):
                    act.wait_ge(gu_done, g + 1)
                    a(silu_g, psum[:, 1, 0:256], ACT.Silu).then_inc(silu_ready, 1)

                def actT_out(g):
                    act.wait_ge(act_turned, g + 1)
                    a(actT[:, :, :].rearrange("p c s -> p (c s)"), psum[:, 2, 0:256], ACT.Copy).then_inc(actT_ready, 1)

                def y_out(n, par):
                    act.wait_ge(y_done, n)
                    act.wait_ge(sem(f"y_stored{par}{L}"), ((n + 1) >> 1) * 32)
                    a(y_sb[par], psum[:, 3, :], ACT.Copy).then_inc(y_copied, 1)
                    act.wait_ge(y_copied, n)
                    for j in range(2):
                        act.dma_start(y_rows[ds(n * BLK - BLK, BLK), j * 512:(j + 1) * 512], y_sb[par][64 * j:64 * j + 64, :])\
                            .then_inc(sem(f"y_stored{par}{L}"), 16)

                act.wait_ge(*at("tab", L))
                act.wait_ge(*at("y_zero", 1))
                for par in range(2):
                    act.sem_inc(sem(f"y_stored{par}{L}"), 32)
                total = act.value_load(tabs[L][0:1, T_TOTAL:T_TOTAL + 1], min_val=N_EXP, max_val=MAXBLK)
                silu(0)
                actT_out(0)
                silu(1)
                y_out(1, 0)
                actT_out(1)
                with act.Fori(1, (total + 1) >> 1) as pair:
                    for par in range(2):
                        g = pair * 2 + par
                        silu(g)
                        y_out(g, 1 - par)
                        actT_out(g)
                y_out(((total + 1) >> 1) * 2, 1)
                act.sem_inc(sem("hold_act"), 1)

            def combine(L):
                S, nt = f"act_comb{L}", q_tokens(L) // P
                for tt in range(nt):
                    act.wait_ge(*at("y_sum", L, tt))
                    if tt == 0:
                        act.wait_ge(*at("tab", L))
                    a(yb[:, tt, :], ya[:, tt, :], ACT.Square, accum_out=rs[:, 20, tt:tt + 1]).then_inc(*mark(S, ("y_sq", L, tt)))
                act.wait_ge(*at("y_sq", L, nt - 1))
                a(rs[:, 21, 0:nt], rs[:, 20, 0:nt], ACT.Ln, scale=1.0 / D, bias=C("eps")).then_inc(*mark(S, ("y_ln", L)))
                act.wait_ge(*at("y_ln", L))
                a(rs[:, 22, 0:nt], rs[:, 21, 0:nt], ACT.Exp, scale=-0.5).then_inc(*mark(S, ("y_rstd", L)))

            act.preload_act_table_set(LN_EXP)
            with nc.allow_non_contiguous_dma(reason="small vectors"):
                act.dma_start(cst[:, :], A["constants"]).then_inc(*mark("dma_const", ("const",), by=16))
                for i, (lo, src) in enumerate([
                        (0, A["norm_g"].rearrange("l i (k p) -> (l i k) p", p=P)),
                        (64, A["mla_q_gain"].rearrange("l (k p) -> (l k) p", p=P)),
                        (68, A["mla_kv_gain"]),
                        (70, A["pool_scale"].rearrange("l (k p) -> (l k) p", p=P))]):
                    act.dma_start(vec_rows[lo:lo + src.shape[0], :], src).then_inc(*mark("dma_vec", by=16))
                act.dma_start(bias_rows[0:96, :], A["ada_b"].rearrange("l (m p) -> (l m) p", p=P))\
                    .then_inc(*mark("dma_vec", ("vec_rows",), by=16))
                act.dma_start(c_sb[:, 0, :], A["c"].rearrange("o (p k) -> p (o k)", p=P)).then_inc(*mark("dma_c", by=16))
                act.dma_start(c_sb[:, 1, :], A["c_ctx"].rearrange("(p k) -> p k", p=P)).then_inc(*mark("dma_c", ("c",), by=16))
                for L in range(DEPTH):
                    for dst, src in ((rt_b[:, L, 0:4], A["router_gb"][L]), (rt_b[:, L, 4:20], A["router_eb"][L]),
                                     (neg_sink[:, L * 4:L * 4 + 4], A["swa_sink"][L]),
                                     (dl[:, L, :, :].rearrange("p a b -> p (a b)"), A["diff_lambda"][L].rearrange("a b -> (a b)")),
                                     (subln[:, L, :], A["diff_subln"][L])):
                        act.dma_start(dst, src.partition_broadcast(P)).then_inc(*mark("dma_rows", by=16))
                    M.name("dma_rows", ("rows", L))

                def small_weights(L, S):
                    act.dma_start(w_uq[:, :, :], A["mla_w_uq"][L].rearrange("(j p) n -> p j n", p=P)).then_inc(*mark(S, by=16))
                    act.dma_start(w_ukv[:, :], A["mla_w_ukv"][L]).then_inc(*mark(S, by=16))
                    act.dma_start(w_rt[:, :, 0:4], A["router_gw"][L].rearrange("(k p) n -> p k n", p=P)).then_inc(*mark(S, by=16))
                    act.dma_start(w_rt[:, :, 4:20], A["router_ew"][L].rearrange("(k p) n -> p k n", p=P)).then_inc(*mark(S, by=16))
                    act.wait_ge(*at("pads"))
                    for g in range(4):
                        lo = 64 * (g % 2)
                        act.dma_start(w_pool[lo:lo + 64, g // 2, lo:lo + 64], A["pool_w"][L, g])\
                            .then_inc(*mark(S, *([("small_w", L)] if g == 3 else []), by=16))

                small_weights(0, "dma_small0")
            act.wait_ge(*at("c"))
            a(c_t[:, :, :], c_sb[:, :, :], ACT.Exp, scale=-1.0).then_inc(*mark("act_start", ("c_exp",)))
            act.wait_ge(*at("lam_dots"))
            a(dlp[:, :, :, 0:1].rearrange("p a b c -> p (a b c)"), dls[:, :], ACT.Exp).then_inc(*mark("act_start", ("lam_exp",)))
            for k in range(KD):
                copy("act_start", xT[:, k, :], ("x0", k))
            for L in range(DEPTH):
                norm(L, 1, NTOK, None if L == 0 else ("x_t", L - 1, KD - 1))
                project(L)
                latent_projections(L)
                mix(L)
                project_out(L)
                norm(L, 2, q_tokens(L), ("x_t", L, KD - 1))
                route(L)
                if L == 0:
                    act.wait_ge(*at("filled", "rk", 0))
                    with nc.allow_non_contiguous_dma(reason="small weights"):
                        small_weights(1, "dma_small1")
                act.preload_act_table(ACT.Silu)
                experts(L)
                act.preload_act_table_set(LN_EXP)
                combine(L)

        @block.vector
        def _(v):
            tt_, ts, stt = nc.vector.tensor_tensor, nc.vector.tensor_scalar, nc.vector.scalar_tensor_tensor
            red = nc.vector.tensor_reduce

            def norm(L, w, n):
                S = f"v_norm{w}{L}"
                v.wait_ge(*at("rstd", (L, w)))
                for k in range(KD):
                    tt_(hT[:, k, 0:n], xT[:, k, 0:n], rstd[:, 0:n], ALU.mult).then_inc(*mark(S, ("xn", L, w, k)))

            def ada_rows(S, L, r):
                v.wait_ge(*at("used", item_no[("ada", L, 4 * r + 3)]))
                if (L, r) != (0, 0):
                    v.wait_ge(*at("filled", "adaT", *((L, r - 1) if r else (L - 1, 2))))
                nc.vector.tensor_copy(ada_sb[:, :], psum[:, B_ADA, :]).then_inc(*mark(S, ("ada_sb", L, r)))

            def ada_columns(S, L, r):
                t = read(v, "adaT", L, r).rearrange("p (q g c) -> p q g c", q=4, g=4)
                for q in range(4):
                    dst = mod[L][:, r * 16:(r + 1) * 16, :].rearrange("p (g q) s -> p q g s", q=4)[:, q, :, :]
                    b = ada_bT[:, L * 48 + r * 16:L * 48 + (r + 1) * 16].rearrange("p (g q) -> p q g", q=4)[:, q, :]
                    ins = tt_(dst, t[:, q, :, 0:2], b.unsqueeze(2).to_broadcast([P, 4, 2]), ALU.add)
                ins.then_inc(*mark(S, ("read", "adaT", L, r)))
                v.wait_ge(*at("read", "adaT", L, r))

                def gains(i):
                    return vecT[:, L * 32 + i * 8:L * 32 + i * 8 + 8].unsqueeze(2).to_broadcast([P, 8, 2])

                if r == 0:
                    stt(amp[L][:, 0, :, :], mod[L][:, 8:16, :], 1.0, gains(0), ALU.add, ALU.mult).then_inc(*mark(S, ("amp", L, 0)))
                elif r == 1:
                    tt_(amp[L][:, 1, :, :], mod[L][:, 16:24, :], gains(1), ALU.mult).then_inc(*mark(S, ("amp", L, 1)))
                else:
                    tt_(amp[L][:, 3, :, :], mod[L][:, 40:48, :], gains(3), ALU.mult)
                    stt(amp[L][:, 2, :, :], mod[L][:, 32:40, :], 1.0, gains(2), ALU.add, ALU.mult).then_inc(*mark(S, ("amp", L, 2)))

            roped = []

            def rope(S, L, name):
                x, kind, lo, hi = ROPES[L][name]
                i = len(roped) % 2
                roped.append((L, name))
                t = read(v, "rot", L, name)[lo:hi, 0:SEQ]
                tt_(rope_s[i][lo:hi, :], t, C("sin_" + kind)[lo:hi, :], ALU.mult).then_inc(*mark(S, ("read", "rot", L, name)))
                v.wait_ge(*at("read", "rot", L, name))
                v.wait_ge(*at("x_cos", L, name))
                tt_(x, rope_c[i][lo:hi, :], rope_s[i][lo:hi, :], ALU.add).then_inc(*mark(S, ("roped", L, name)))

            def latents(L):
                S, nq = f"v_lat{L}", q_tokens(L)
                v.wait_ge(*at("rstd", ("cq", L)))
                for j in range(2):
                    stt(cq[:, j, 0:nq], cq[:, j, 0:nq], vecT[:, 64 + 2 * L + j:65 + 2 * L + j], rstd[:, 0:nq], ALU.mult, ALU.mult)\
                        .then_inc(*mark(S, *([("cqn", L)] if j else [])))
                v.wait_ge(*at("rstd", ("ckv", L)))
                stt(ckv, ckv, vecT[:, 68 + L:69 + L], rstd[:, :], ALU.mult, ALU.mult).then_inc(*mark(S, ("ckvn", L)))
                rope(S, L, "kr")
                v.wait_ge(*at("roped", L, "kr"))
                for h in range(HEADS):
                    nc.vector.tensor_copy(kas[L][64:96, h, :], kr[64:96, :]).then_inc(*mark(S, ("kr_out", L, h)))
                for name in ("bk", "bq0", "bq1", "qa0", "qa1", "qa2", "qa3"):
                    rope(S, L, name)
                for j in range(2):
                    rope(S, L, f"dq{j}")
                    v.wait_ge(*at("roped", L, f"dq{j}"))
                    ts(dqs[L][:, j, 1, 0:nq], dqs[L][:, j, 0, 0:nq], C("parity")[:, 1:2], None, ALU.mult).then_inc(*mark(S, ("dq_odd", L, j)))
                    ts(dqs[L][:, j, 0, 0:nq], dqs[L][:, j, 0, 0:nq], C("parity")[:, 0:1], None, ALU.mult).then_inc(*mark(S, ("dq_split", L, j)))
                    rope(S, L, f"dk{j}")

            def mix(L):
                S = f"v_mix{L}"
                U, nq = units(L), q_tokens(L)
                per = len(U) // 3
                ada = ada_plan(L)

                def maxima(u):
                    kind, qt, h = U[u]
                    nk = NTOK if qt < 2 else SEQ
                    s_ = st[:, u % 8, :]
                    if u >= 8:
                        v.wait_ge(*at("read", "s", L, u - 8, 1 if U[u - 8][0] == "diff" else 0))
                        if U[u - 8][0] == "swa":
                            v.wait_ge(*at("sink", L, u - 8))
                    for j in range(2 if kind == "diff" else 1):
                        ins = red(s_[:, j:j + 1], read(v, "s", L, u, j)[:, 0:nk], AX.X, ALU.max, negate=True)
                    if kind == "swa":
                        ins.then_inc(*mark(S, ("smax", L, u)))
                        v.wait_ge(*at("smax", L, u))
                        ins = tt_(s_[:, 0:1], s_[:, 0:1], neg_sink[:, L * 4 + h:L * 4 + h + 1], ALU.min)
                    ins.then_inc(*mark(S, ("nmax", L, u)))

                def weigh(u):
                    kind, qt, h = U[u]
                    nk = NTOK if qt < 2 else SEQ
                    s_ = st[:, u % 8, :]
                    v.wait_ge(*at("read", "s", L, u, 1 if kind == "diff" else 0))
                    if kind == "swa":
                        v.wait_ge(*at("sink", L, u))
                        tt_(s_[:, 2:3], s_[:, 2:3], s_[:, 4:5], ALU.add).then_inc(*mark(S, ("denom", L, u)))
                        v.wait_ge(*at("denom", L, u))
                    if kind == "diff":
                        nc.vector.reciprocal(s_[:, 5:6], s_[:, 3:4]).then_inc(*mark(S, ("r1", L, u)))
                        v.wait_ge(*at("r1", L, u))
                        stt(s_[:, 6:7], s_[:, 2:3], s_[:, 5:6], neg_lam[:, L:L + 1], ALU.mult, ALU.mult).then_inc(*mark(S, ("c1", L, u)))
                        v.wait_ge(*at("c1", L, u))
                        stt(prob[u % 3][:, 0:nk], prob[3][:, 0:nk], s_[:, 6:7], prob[u % 3][:, 0:nk], ALU.mult, ALU.add)\
                            .then_inc(*mark(S, ("prob", L, u)))
                    nc.vector.reciprocal(s_[:, 7:8], s_[:, 2:3]).then_inc(*mark(S, ("rinv", L, u)))

                def outputs(u):
                    kind, qt, h = U[u]
                    o_ = om[KINDS.index(kind) % 2]
                    keys = [("om", L, kind)] if u % per == per - 1 and kind != "diff" else []
                    if kind == "diff" and u % per == 0:
                        v.wait_ge(*at("filled", "mT", L, "mla", 1))
                    t = read(v, "o", L, u)
                    v.wait_ge(*at("rinv", L, u))
                    ts(o_[:, qt, h * 64:h * 64 + 64], t[:, 0:64], st[:, u % 8, 7:8], None, ALU.mult)\
                        .then_inc(*mark(S, ("read", "o", L, u), *keys))

                done = 0
                for i in range(len(U) + 4):
                    if i < len(U):
                        maxima(i)
                    if 1 <= i < len(U) + 1:
                        weigh(i - 1)
                    if i >= 4:
                        outputs(i - 4)
                    while done < len(ada) and done * len(U) <= (i - 1) * len(ada):
                        _, la, ia = ada[done]
                        if ia % 4 == 3:
                            ada_rows(S, la, ia // 4)
                        if ia % 4 == 1 and (la, ia) != (0, 5):
                            ada_columns(S, *((la, ia // 4 - 1) if ia // 4 else (la - 1, 2)))
                        done += 1
                if ada:
                    assert done == len(ada)
                    ada_columns(S, 1, 2)
                q = nq // P
                o_ = om[0][:, 0:q, :]
                v.wait_ge(*at("read", "o", L, len(U) - 1))
                v.wait_ge(*at("filled", "mT", L, "swa", 1))
                tmp = om[1][:, 0:q, :]
                tt_(tmp, o_, o_, ALU.mult).then_inc(*mark(S, ("osq", L)))
                v.wait_ge(*at("osq", L))
                red(dstat[:, 0:q, 0:4], tmp.rearrange("p q (h c) -> p q h c", h=HEADS), AX.X, ALU.add).then_inc(*mark(S, ("dsum", L)))
                v.wait_ge(*at("drstd", L))
                for i in range(q):
                    tt_(o_[:, i, :].rearrange("p (h c) -> p h c", h=HEADS), o_[:, i, :].rearrange("p (h c) -> p h c", h=HEADS),
                        dstat[:, i, 8:12].unsqueeze(2).to_broadcast([P, HEADS, 64]), ALU.mult).then_inc(*mark(S, ("on", L, i)))
                for i in range(q):
                    v.wait_ge(*at("on", L, i))
                    ins = tt_(o_[:, i, :].rearrange("p (h c) -> p h c", h=HEADS), o_[:, i, :].rearrange("p (h c) -> p h c", h=HEADS),
                              subln[:, L, :].unsqueeze(1).to_broadcast([P, HEADS, 64]), ALU.mult)
                ins.then_inc(*mark(S, ("om", L, "diff")))

            def add_out(L):
                S, nq = f"v_out{L}", q_tokens(L)
                v.wait_ge(*at("rstd", ("o", L)))
                for k in range(KD):
                    v.wait_ge(*at("read", "oT", L, k))
                    tt_(oT[:, k, 0:nq], oT[:, k, 0:nq], rstd[:, 0:nq], ALU.mult).then_inc(*mark(S, ("x_t", L, k)))
                for k in range(KD):
                    v.wait_ge(*at("x_t", L, k))
                    tt_(xT[:, k, 0:nq], xT[:, k, 0:nq], oT[:, k, 0:nq], ALU.add).then_inc(*mark(S, ("x", L, 1, k)))

            def route(L):
                S, nt = f"v_route{L}", q_tokens(L) // P
                n = [0]

                def step(ins, *keys):
                    n[0] += 1
                    ins.then_inc(*mark(S, ("step", L, n[0]), *keys))
                    v.wait_ge(*at("step", L, n[0]))

                def b4(x):
                    return x.unsqueeze(2).to_broadcast([P, nt, 4])

                def s1(i):
                    return rs[:, i, 0:nt]

                first = C("first").unsqueeze(1).to_broadcast([P, nt, 4])

                def first_max(x, top, out_, tmp, is_shifted=False):
                    step(tt_(tmp, x, b4(top), ALU.is_equal))
                    step(tt_(tmp, tmp, first, ALU.mult))
                    step(red(s1(30), tmp, AX.X, ALU.max))
                    step(tt_(out_, tmp, b4(s1(30)), ALU.is_equal))

                t = read(v, "lg", L)[:, 0:nt * 20].rearrange("p (t c) -> p t c", t=nt)
                step(tt_(lg[:, 0:nt, :], t, rt_b[:, L, :].unsqueeze(1).to_broadcast([P, nt, 20]), ALU.add), ("read", "lg", L))
                g_, e_ = lg[:, 0:nt, 0:4], lg[:, 0:nt, 4:20].rearrange("p t (g j) -> p t g j", g=4)
                R4 = [r4[:, i, 0:nt, :] for i in range(10)]
                step(red(s1(0), g_, AX.X, ALU.max))
                step(tt_(R4[0], g_, b4(s1(0)), ALU.subtract), ("g_shift", L))
                first_max(g_, s1(0), R4[2], R4[3])
                m = r16[:, 5, 0:nt, :].rearrange("p t (g j) -> p t g j", g=4)
                for i in range(nt):
                    ins = tt_(m[:, i], e_[:, i], R4[2][:, i].unsqueeze(2).to_broadcast([P, 4, 4]), ALU.mult)
                step(ins)
                step(red(R4[4], m.rearrange("p t g j -> p t j g"), AX.X, ALU.add))
                step(red(s1(1), R4[4], AX.X, ALU.max))
                first_max(R4[4], s1(1), R4[5], R4[3])
                step(stt(R4[6], R4[5], NEG, R4[4], ALU.mult, ALU.add))
                step(red(s1(2), R4[6], AX.X, ALU.max))
                step(tt_(s1(6), s1(2), s1(1), ALU.subtract), ("top_diff", L))
                first_max(R4[6], s1(2), R4[7], R4[3])
                for which, oh in ((0, R4[5]), (1, R4[7])):
                    for i in range(nt):
                        ins = tt_(r16[:, which, i, :].rearrange("p (g j) -> p g j", g=4),
                                  R4[2][:, i].unsqueeze(2).to_broadcast([P, 4, 4]),
                                  oh[:, i].unsqueeze(1).to_broadcast([P, 4, 4]), ALU.mult)
                    step(ins)
                step(tt_(chosen[:, 4 - nt:4, :], r16[:, 0, 0:nt, :], r16[:, 1, 0:nt, :], ALU.add), ("chosen", L))
                v.wait_ge(*at("g_exp", L))
                step(red(s1(3), R4[1], AX.X, ALU.add))
                step(nc.vector.reciprocal(s1(4), s1(3)))
                v.wait_ge(*at("top_exp", L))
                step(ts(s1(5), s1(7), 1.0, None, ALU.add))
                step(nc.vector.reciprocal(s1(8), s1(5)))
                step(tt_(s1(9), s1(8), s1(4), ALU.mult))
                step(tt_(s1(10), s1(9), s1(7), ALU.mult), ("weights", L))
                t = read(v, "rk", L)
                step(nc.vector.tensor_copy(e16[:, 0, :], t[:, nt * 16:nt * 16 + 16]))
                step(tt_(cmp7[:, :, :], e16[:, 0, :].unsqueeze(2).to_broadcast([P, 16, 7]),
                         C("more").unsqueeze(1).to_broadcast([P, 16, 7]), ALU.is_ge))
                step(red(e16[:, 1, :], cmp7[:, :, :], AX.X, ALU.add))
                step(ts(e16[:, 1, :], e16[:, 1, :], 1.0, None, ALU.add))
                step(nc.vector.tensor_tensor_scan(e16[:, 2, :], ones[:, 0:16], e16[:, 1, :], 0.0, ALU.mult, ALU.add))
                step(tt_(e16[:, 3, :], e16[:, 2, :], e16[:, 1, :], ALU.subtract))
                step(ts(e16[:, 4, :], e16[:, 3, :], float(BLK), None, ALU.mult))
                for off, i in ((T_NB, 1), (T_START, 3), (T_CUM, 2)):
                    nc.vector.tensor_copy(tabs[L][:, off:off + 16], e16[:, i, :])
                step(nc.vector.tensor_copy(tabs[L][:, T_TOTAL:T_TOTAL + 1], e16[:, 2, 15:16]), ("tab", L))
                for i in range(nt):
                    ins = tt_(r16[:, 3, i, :], t[:, i * 16:i * 16 + 16], e16[:, 4, :], ALU.add)
                step(ins, ("read", "rk", L))
                for which in range(2):
                    step(tt_(r16[:, 4, 0:nt, :], r16[:, 3, 0:nt, :], r16[:, which, 0:nt, :], ALU.mult))
                    step(red(s1(11 + which), r16[:, 4, 0:nt, :], AX.X, ALU.add))
                step(nc.vector.tensor_copy(spos[:, :, 0:nt], rs[:, 11:13, 0:nt]), ("spos", L))
                ts(spos_t[:, 0, :, 0:nt], spos[:, :, 0:nt], BLK - 1, None, ALU.bitwise_and)
                step(ts(spos_t[:, 1, :, 0:nt], spos[:, :, 0:nt], 6, None, ALU.logical_shift_right))
                step(nc.vector.tensor_copy(spos_f[:, :, :, 0:nt], spos_t[:, :, :, 0:nt]))
                for which in range(2):
                    w = slice(which * nt, (which + 1) * nt)
                    tt_(place_hot[:, w, :], spos_f[:, 0, which, 0:nt].unsqueeze(2).to_broadcast([P, nt, BLK]),
                        C("count")[:, 0:BLK].unsqueeze(1).to_broadcast([P, nt, BLK]), ALU.is_equal)
                    step(tt_(block_id[:, w, :], spos_f[:, 1, which, 0:nt].unsqueeze(2).to_broadcast([P, nt, COLS]),
                             C("count")[:, 0:COLS].unsqueeze(1).to_broadcast([P, nt, COLS]), ALU.is_equal))
                    step(tt_(block_id[:, w, :], block_id[:, w, :], C("token")[:, 0:nt].unsqueeze(2).to_broadcast([P, nt, COLS]), ALU.mult),
                         *([("slot_hot", L)] if which else []))
                t = read(v, "st", L)
                nc.vector.tensor_copy(slots[:, :], t[0:BLK, 0:COLS]).then_inc(*mark(S, ("read", "st", L), ("slots", L)))

            def experts(L):
                x_turned, x_ready = sem(f"x_turned{L}"), sem(f"x_ready{L}")
                silu_ready, act_ready = sem(f"silu_ready{L}"), sem(f"act_ready{L}")

                def x_out():
                    return nc.vector.tensor_copy(xgT[:, :, :].rearrange("p k s -> p (k s)"), psum[:, 0, :]).then_inc(x_ready, 1)

                total = v.value_load(tabs[L][0:1, T_TOTAL:T_TOTAL + 1], min_val=N_EXP, max_val=MAXBLK)
                v.wait_ge(x_turned, 1)
                x_out()
                with v.Fori(0, (total + 1) >> 1) as pair:
                    for par in range(2):
                        g = pair * 2 + par
                        v.wait_ge(silu_ready, g + 1)
                        tt_(act_rows, silu_g, psum[:, 1, 256:512], ALU.mult).then_inc(act_ready, 1)
                        v.wait_ge(x_turned, g + 2)
                        x_out()
                v.wait_ge(x_ready, ((total + 1) >> 1) * 2 + 1)
                nc.vector.memset(rs[:, 31, 0:1], 0.0).then_inc(*mark(f"v_comb{L}", ("banks_out", L)))

            def combine(L):
                S, nt = f"v_comb{L}", q_tokens(L) // P
                for tt in range(nt):
                    v.wait_ge(*at("y_gathered", L, tt))
                    ts(ya[:, tt, :], ya[:, tt, :], rs[:, 9, tt:tt + 1], None, ALU.mult).then_inc(*mark(S, ("y1", L, tt)))
                    v.wait_ge(*at("y1", L, tt))
                    stt(ya[:, tt, :], yb[:, tt, :], rs[:, 10, tt:tt + 1], ya[:, tt, :], ALU.mult, ALU.add).then_inc(*mark(S, ("y_sum", L, tt)))
                v.wait_ge(*at("y_rstd", L))
                for tt in range(nt):
                    ts(ya[:, tt, :], ya[:, tt, :], rs[:, 22, tt:tt + 1], None, ALU.mult).then_inc(*mark(S, ("y_norm", L, tt)))
                for k in range(KD):
                    t = read(v, "yT", L, k)
                    for s, lo, hi in streams(nt * P):
                        ins = stt(xT[:, k, lo:hi], t[:, lo:hi], amp[L][:, 3, k, s:s + 1], xT[:, k, lo:hi], ALU.mult, ALU.add)
                    ins.then_inc(*mark(S, ("read", "yT", L, k), ("x", L, 2, k)))

            S0 = "v_start"
            nc.vector.memset(ones[:, :], 1.0).then_inc(*mark(S0, ("ones",)))
            for j in range(2):
                nc.vector.memset(up[j][:, :, :], 0.0)
            nc.vector.memset(w_pool[:, :, :], 0.0).then_inc(*mark(S0, ("pads",)))
            nc.vector.memset(silu_c[:, :, :], 0.0).then_inc(*mark(S0, ("silu_zero",)))
            nc.vector.memset(chosen[:, :, :], 0.0)
            v.wait_ge(*at("const"))
            nc.vector.tensor_copy(band[:, :], C("band"))
            nc.vector.tensor_copy(ident16[:, :], ident).then_inc(*mark(S0, ("band",)))
            t = read(v, "vec")
            nc.vector.tensor_copy(vecT[:, :], t[:, 0:74])
            nc.vector.tensor_copy(ada_bT[:, :], t[:, P:P + 96]).then_inc(*mark(S0, ("read", "vec")))
            v.wait_ge(*at("c_exp"))
            ts(c_t[:, :, :], c_t[:, :, :], 1.0, None, ALU.add).then_inc(*mark(S0, ("c1",)))
            v.wait_ge(*at("c1"))
            nc.vector.reciprocal(c_t[:, :, :], c_t[:, :, :]).then_inc(*mark(S0, ("c2",)))
            v.wait_ge(*at("c2"))
            v.wait_ge(*at("silu_zero"))
            tt_(silu_c[:, :, 0:2].rearrange("p k s -> p s k"), c_sb[:, :, :], c_t[:, :, :], ALU.mult).then_inc(*mark(S0, ("silu_c",)))
            v.wait_ge(*at("rows", DEPTH - 1))
            ts(neg_sink[:, :], neg_sink[:, :], -1.0, None, ALU.mult)
            for L in range(DEPTH):
                ts(subln[:, L, :], subln[:, L, :], 1.0 - LAM_INIT[L], None, ALU.mult)
            d = dl[:, :, :, :].rearrange("p l (a b) c -> p l a b c", b=2)
            for L in range(DEPTH):
                ins = tt_(dlp[:, L, :, :], d[:, L, :, 0, :], d[:, L, :, 1, :], ALU.mult)
            ins.then_inc(*mark(S0, ("lam_prod",)))
            v.wait_ge(*at("lam_prod"))
            red(dls[:, :], dlp[:, :, :, :].rearrange("p l a c -> p (l a) c"), AX.X, ALU.add).then_inc(*mark(S0, ("lam_dots",)))
            v.wait_ge(*at("lam_exp"))
            for L in range(DEPTH):
                ins = stt(neg_lam[:, L:L + 1], dlp[:, L, 1, 0:1], -LAM_INIT[L], dlp[:, L, 0, 0:1], ALU.add, ALU.subtract)
            ins.then_inc(*mark(S0, ("neg_lam",)))
            ada_rows(S0, 0, 0)
            ada_columns(S0, 0, 0)
            for L in range(DEPTH):
                norm(L, 1, NTOK)
                latents(L)
                mix(L)
                add_out(L)
                norm(L, 2, q_tokens(L))
                route(L)
                experts(L)
                combine(L)
            for tt in range(2):
                for half in range(2):
                    t = read(v, "fin", tt, half)
                    nc.vector.tensor_copy(rows[:, tt, half * 512:half * 512 + 512], t).then_inc(*mark("v_fin", ("read", "fin", tt, half)))

        @block.gpsimd
        def _(g_):
            gt = nc.gpsimd.tensor_tensor

            def cosines(L):
                S = f"g_rope{L}"
                order = ["kr", "bk", "bq0", "bq1", "qa0", "qa1", "qa2", "qa3", "dq0", "dk0", "dq1", "dk1"]
                for n, name in enumerate(order):
                    x, kind, lo, hi = ROPES[L][name]
                    g_.wait_ge(*at("tile", L, name))
                    if n:
                        g_.wait_ge(*at("x_cos", L, order[n - 1]))
                    if n >= 2:
                        g_.wait_ge(*at("roped", L, order[n - 2]))
                    gt(rope_c[n % 2][lo:hi, :], x, C("cos_" + kind)[lo:hi, :], ALU.mult).then_inc(*mark(S, ("x_cos", L, name)))

            def pooling(L, j):
                S, ns = f"g_pool{L}", q_tokens(L) // SEQ
                n = [0]

                def step(ins, *keys):
                    n[0] += 1
                    ins.then_inc(*mark(S, ("pstep", L, j, n[0]), *keys))
                    g_.wait_ge(*at("pstep", L, j, n[0]))

                def widen(dst, src, lo, hi, half, r=0):
                    step(gt(dst[r:, 0:ns, lo:hi], src[r:, 0:ns, lo - half:hi - half], src[r:, 0:ns, lo + half:hi + half], ALU.add))

                g_.wait_ge(*at("read", f"u{j}", L))
                if j == 0:
                    g_.wait_ge(*at("x_cos", L, "dk1"))
                step(gt(pa[:, 0:ns, 1:PADW], up[j][:, 0:ns, 0:PADW - 1], up[j][:, 0:ns, 1:PADW], ALU.add))
                if j == 0:
                    widen(pb, pa, 2, PADW - 2, 1, 64)
                else:
                    widen(pb, pa, 2, PADW - 2, 1)
                    widen(pa, pb, 4, PADW - 4, 2)
                    widen(pb, pa, 8, PADW - 8, 4, 64)
                d = dgs[L][:, j, :].rearrange("p (s t) -> p s t", s=2)
                for r, src in ((0, pa), (64, pb)):
                    for s in range(ns):
                        step(gt(d[r:r + 64, s, :], src[r:r + 64, s, 16:16 + SEQ], inv_count[r:r + 64, j, :], ALU.mult))
                step(gt(d[:, 0:ns, :], d[:, 0:ns, :], up[j][:, 0:ns, 16:16 + SEQ], ALU.subtract), ("dg", L, j))

            def route(L):
                S, nt = f"g_route{L}", q_tokens(L) // P
                for tt in range(nt):
                    g_.wait_ge(*at("h_tile", L, tt))
                    g_.dma_start(h_rows[L][tt * P:(tt + 1) * P, :], rows[:, tt, :]).then_inc(*mark(f"dma_h{L}", ("h_stored", L, tt), by=16))

            def experts(L):
                x_rows, x_turned, col_ready = sem(f"x_rows{L}"), sem(f"x_turned{L}"), sem(f"col_ready{L}")
                g_.wait_ge(*at("slots", L))
                g_.wait_ge(*at("h_stored", L, q_tokens(L) // P - 1))

                def gather(g, par, to):
                    nc.gpsimd.tensor_copy(slot_col[:, par:par + 1], slots[:, ds(g, 1)]).then_inc(col_ready, 1)
                    g_.wait_ge(col_ready, g + 1)
                    g_.sem_inc(sem("hold"), 1)
                    g_.indirect_dma_start(to, None, h_rows[L], bass.IndirectOffsetOnAxis(ap=slot_col[:, par:par + 1], axis=0))\
                        .then_inc(sem(f"gathered{par}{L}"), 16)

                def pass_on(g, par):
                    g_.wait_ge(sem(f"gathered{par}{L}"), ((g >> 1) + 1) * 16)
                    if not isinstance(g, int) or g:
                        g_.wait_ge(x_turned, g)
                    g_.sem_inc(sem("hold"), 1)
                    nc.gpsimd.tensor_copy(xg, xg_in[par]).then_inc(x_rows, 1)
                    g_.wait_ge(x_rows, g + 1)

                gather(0, 0, xg)
                gather(1, 1, xg_in[1])
                g_.wait_ge(*at("tab", L))
                total = g_.value_load(tabs[L][0:1, T_TOTAL:T_TOTAL + 1], min_val=N_EXP, max_val=MAXBLK)
                pairs = (total >> 1) + 1
                g_.wait_ge(sem(f"gathered0{L}"), 16)
                g_.sem_inc(x_rows, 1)
                gather(2, 0, xg_in[0])
                pass_on(1, 1)
                gather(3, 1, xg_in[1])
                with g_.Fori(1, pairs - 1) as pair:
                    for par in range(2):
                        pass_on(pair * 2 + par, par)
                        gather(pair * 2 + (par + 2), par, xg_in[par])
                pass_on(pairs * 2 - 2, 0)
                pass_on(pairs * 2 - 1, 1)
                for par in range(2):
                    g_.wait_ge(sem(f"y_stored{par}{L}"), ((total + 1) >> 1) * 32 + 32)
                g_.sem_inc(sem("hold"), 1)
                g_.wait_ge(*at("banks_out", L))
                for tt in range(q_tokens(L) // P):
                    for which, dst in ((0, ya), (1, yb)):
                        g_.indirect_dma_start(dst[:, tt, :], None, y_rows,
                                              bass.IndirectOffsetOnAxis(ap=spos[:, which, tt:tt + 1], axis=0))\
                            .then_inc(*mark(f"dma_y{L}{tt}", *([("y_gathered", L, tt)] if which else []), by=16))

            nc.gpsimd.memset(zeros[:, :], 0.0).then_inc(*mark("g_start", ("zeros",)))
            g_.wait_ge(*at("zeros"))
            g_.wait_ge(*at("const"))
            for L in range(DEPTH):
                cosines(L)
                pooling(L, 0)
                pooling(L, 1)
                if L == 0:
                    for half in range(2):
                        g_.dma_start(y_rows.rearrange("(p n) (h d) -> p n h d", p=P, h=2)[:, :, half, :],
                                     zeros[:, :].unsqueeze(1).to_broadcast([P, y_rows.shape[0] // P, D // 2]))\
                            .then_inc(*mark("dma_y_zero", ("y_zero", half), by=16))
                route(L)
                experts(L)

        @block.sync
        def _(sp):
            def load(n):
                it = items[n]
                if n >= (3 if n < n_stage0 else n_stage0 + 3):
                    sp.wait_ge(*at("used", n - 3))
                sp.dma_start(staged(it) if it[0] != "ada" else stage_buffer(n).rearrange("p (k c) -> p k c", k=2), stage_source(it))\
                    .then_inc(*mark(f"dma_stage{n % 3}", ("staged", n), by=16))

            def expert(L, e, par):
                gu = A["exp_w_gu"][L].rearrange("e (k p) n -> e p k n", p=P)
                dn = A["exp_w_down"][L].rearrange("e (k p) n -> e p k n", p=P)

                def pick(x):
                    return x[e] if isinstance(e, int) else x[ds(e, 1), :, :, :].squeeze(0)

                place = (par + L) % 2
                for i in range(2):
                    sp.dma_start(w_gu_in[place][:, 4 * i:4 * i + 4, :], pick(gu)[:, 4 * i:4 * i + 4, :]).then_inc(sem(f"w_gu{place}"), 16)
                return lambda: sp.dma_start(w_dn[place], pick(dn)).then_inc(sem(f"w_dn{place}"), 16)

            sp.dma_start(rows[:, 0:2, :], A["x"][0].rearrange("(t p) d -> p t d", p=P)).then_inc(*mark("dma_x", by=16))
            sp.dma_start(rows[:, 2:4, :], A["ctx"][0].rearrange("(t p) d -> p t d", p=P)).then_inc(*mark("dma_x", ("x_rows",), by=16))
            for L in range(DEPTH):
                lo, hi = (0, n_stage0) if L == 0 else (n_stage0, len(items))
                if L:
                    cum = sp.value_load(tabs[L - 1][0:1, T_CUM + N_EXP - 2:T_CUM + N_EXP - 1], min_val=1, max_val=MAXBLK)
                    sp.wait_ge(sem(f"gu_done{L - 1}"), cum)
                    sp.sem_inc(sem("sp_hold"), 1)
                    for n in range(lo, lo + 2):
                        load(n)
                    sp.wait_ge(sem(f"y_done{L - 1}"), cum)
                    sp.sem_inc(sem("sp_hold"), 1)
                    lo += 2
                for n in range(lo, hi):
                    load(n)
                sp.wait_ge(*at("filled", "mT", L, "diff", 1))
                sp.wait_ge(*at("filled", "pool", L, 1))
                expert(L, 0, 0)()
                for n in (hi - 2, hi - 1):
                    sp.wait_ge(*at("used", n))
                expert(L, 1, 1)()
                sp.wait_ge(*at("tab", L))
                with sp.Fori(1, N_EXP // 2) as pair:
                    for par in range(2):
                        cum = sp.value_load(tabs[L][0:1, ds(pair * 2 + (T_CUM - 2 + par), 1)], min_val=1, max_val=MAXBLK)
                        sp.wait_ge(sem(f"gu_done{L}"), cum)
                        down = expert(L, pair * 2 + par, par)
                        sp.wait_ge(sem(f"y_done{L}"), cum)
                        down()
            for tt in range(2):
                for half in range(2):
                    sp.wait_ge(*at("read", "fin", tt, half))
                sp.dma_start(out[0, tt * P:(tt + 1) * P, :], rows[:, tt, :]).then_inc(*mark("dma_out", by=16))
            sp.wait_ge(sem("dma_out"), 32)
        return M


_INS = ['x', 'c', 'ctx', 'c_ctx', 'ada_w', 'ada_b', 'norm_g', 'w_in', 'mla_q_gain', 'mla_kv_gain', 'mla_w_uq',
        'mla_w_ukv', 'swa_sink', 'diff_lambda', 'diff_subln', 'pool_w', 'pool_scale', 'w_out', 'router_gw',
        'router_gb', 'router_ew', 'router_eb', 'exp_w_gu', 'exp_w_down']


def kernel(**inputs):
    import numpy as _np
    import concourse.bacc as _bacc
    from concourse import mybir as _mybir
    from concourse.bass_utils import run_bass_kernel_spmd as _run

    arrays = {f"in_{name}_dram": _np.ascontiguousarray(inputs[name]) for name in _INS}
    arrays["in_constants_dram"] = CONSTANTS

    def build(known):
        nc = _bacc.Bacc("TRN2", target_bir_lowering=False, num_devices=1)
        args = {n[3:-5]: nc.dram_tensor(n, a.shape, _mybir.dt.from_np(a.dtype), kind="ExternalInput").ap()
                for n, a in arrays.items()}
        out = nc.dram_tensor("out_0_dram", (1, SEQ, D), _mybir.dt.float32, kind="ExternalOutput").ap()
        return nc, hybrid_block(nc, args, out, known)

    _, counts = build(None)
    nc, _ = build(counts)
    r = _run(nc, [arrays], core_ids=[0])
    return r.results[0]["out_0_dram"]
```

```python
import concourse.bass as bass
from concourse import mybir
from contextlib import ExitStack
import numpy as np

F32 = mybir.dt.float32
BF16 = mybir.dt.bfloat16
I32 = mybir.dt.int32
ALU = mybir.AluOpType
ACT = mybir.ActivationFunctionType
AX = mybir.AxisListType
ds = bass.ds

P = 128
D = 1024
KD = D // P
SEQ = 256
NTOK = 512
DEPTH = 2
GRID_W = 64
EPS = 1e-6
HEADS = 4
MLA_NOPE, MLA_ROPE, MLA_V = 64, 32, 64
MLA_QK = MLA_NOPE + MLA_ROPE
MLA_SCALE = MLA_QK ** -0.5
SWA_D, SWA_WINDOW = 64, 128
SWA_SCALE = SWA_D ** -0.5
DIFF_QK = 32
DIFF_SCALE = DIFF_QK ** -0.5
N_EXP, N_GRP, PER_GRP, F_EXP = 16, 4, 4, 512
BLK = 64
MAXBLK = (2 * NTOK + N_EXP * (BLK - 1)) // BLK
COLS = MAXBLK + 3
LAM_INIT = [0.8 - 0.6 * float(np.exp(-0.3 * L)) for L in range(DEPTH)]
NEG = -1e30
LN_EXP = "natural_log_exp_and_others"

C_CQ, C_CKV, C_KR, C_BQ, C_BK, C_BV, C_DQ, C_DK, C_DV, C_U, C_END = (
    0, 256, 384, 416, 672, 800, 928, 1184, 1440, 1696, 1952)
IN_CHUNKS = [(C_CQ, C_BQ), (C_BQ, C_DQ), (C_DQ, C_DV), (C_DV, C_END)]

CST = {}


def constants():
    cols, parts = 0, []

    def put(name, a):
        nonlocal cols
        full = np.zeros((P, a.shape[1]), np.float32)
        full[:a.shape[0]] = a
        CST[name] = (cols, cols + a.shape[1])
        cols += a.shape[1]
        parts.append(full)

    def rot(dim, start, stop):
        r, h = np.zeros((P, P), np.float32), dim // 2
        for b in range(start, stop, dim):
            for i in range(h):
                r[b + i + h, b + i] = -1.0
                r[b + i, b + i + h] = 1.0
        return r

    def rope(dim, start, stop):
        rows = SEQ // GRID_W
        row = np.repeat(np.arange(rows), GRID_W).astype(np.float32)
        col = np.tile(np.arange(GRID_W), rows).astype(np.float32)
        n = dim // 4
        inv = (10000.0 ** (-np.arange(n, dtype=np.float32) / n)).astype(np.float32)
        ang = np.concatenate([row[:, None] * inv, col[:, None] * inv], -1)
        c, s = np.ones((P, SEQ), np.float32), np.zeros((P, SEQ), np.float32)
        for b in range(start, stop, dim):
            for i in range(dim):
                c[b + i] = np.cos(ang[:, i % (dim // 2)])
                s[b + i] = np.sin(ang[:, i % (dim // 2)])
        return c, s

    put("ident", np.eye(P))
    put("eps", np.full((P, 1), EPS))
    CST["soon"] = (0, cols)
    for name, dim, a, b in (("mla", MLA_ROPE, MLA_NOPE, MLA_QK), ("swa", SWA_D, 0, P), ("diff", DIFF_QK, 0, P)):
        put("rot_" + name, rot(dim, a, b))
        c, s = rope(dim, a, b)
        put("cos_" + name, c)
        put("sin_" + name, s)
    t = np.arange(SEQ)
    inv_count = np.zeros((P, 2, SEQ), np.float32)
    for g, w in enumerate((2, 4, 8, 16)):
        cnt = np.minimum(t - w // 2 + w, SEQ) - np.maximum(t - w // 2, 0)
        inv_count[64 * (g % 2):64 * (g % 2) + 64, g // 2] = 1.0 / cnt
    put("inv_count", inv_count.reshape(P, -1))
    put("before", np.triu(np.ones((P, P)), 1))
    q, k = np.arange(P)[:, None], np.arange(SEQ)[None]
    put("band", np.concatenate([np.where(np.abs(k - q - P * i) <= SWA_WINDOW, 0.0, NEG) for i in range(2)], 1))
    put("more", np.tile(BLK * np.arange(1, 8) + 1, (P, 1)))
    put("count", np.tile(np.arange(BLK), (P, 1)))
    for layer, tiles in ((0, 4), (1, 2)):
        put(f"token{layer}", np.tile(np.arange(P)[:, None] + P * np.arange(tiles)[None], (1, 2)))
    put("first", np.tile(4.0 - np.arange(4), (P, 1)))
    half = (np.arange(P) // DIFF_QK) % 2
    put("parity", np.stack([1 - half, half], 1))
    return np.concatenate(parts, 1)


CONSTANTS = constants()


class Marks:

    def __init__(self, nc, ctx, known):
        self.nc, self.ctx, self.known = nc, ctx, known
        self.sems, self.count, self.where, self.bank_of = {}, {}, {}, {}

    def sem(self, name):
        if name not in self.sems:
            self.sems[name] = self.ctx.enter_context(self.nc.semaphore(name))
        return self.sems[name]

    def mark(self, family, *keys, by=1):
        self.count[family] = self.count.get(family, 0) + by
        for key in keys:
            assert key not in self.where, key
            self.where[key] = (family, self.count[family])
        return self.sem(family), by

    def name(self, family, key):
        self.where[key] = (family, self.count[family])

    def at(self, *key):
        if self.known is None:
            return self.sem("unknown"), 1
        family, n = self.known.where[key]
        return self.sem(family), n

    def bank(self, *job):
        return (self.known or self).bank_of.get(job, 0)


def hybrid_block(nc, A, out, known=None):
    ctx = ExitStack()
    with ctx:
        M = Marks(nc, ctx, known)
        mark, at, sem = M.mark, M.at, M.sem

        def sb(name, shape, dt=F32):
            return ctx.enter_context(nc.sbuf_tensor(name, shape, dt))

        def scratch(name, shape, dt=F32):
            return nc.dram_tensor(name, shape, dt, kind="Internal").ap()

        h_rows = [scratch(f"h_rows{L}", (NTOK if L == 0 else SEQ, D)) for L in range(DEPTH)]
        y_rows = scratch("y_rows", (BLK * (MAXBLK + 1), D))

        EXP_W = 12 * D
        W = [sb(f"weights{i}", [P, EXP_W]) for i in range(2)]
        w_gu = [W[i][:, 0:8 * D].rearrange("p (k c h n) -> p k h c n", k=KD, c=2, h=2) for i in range(2)]
        w_gu_in = [W[i][:, 0:8 * D].rearrange("p (k n) -> p k n", k=KD) for i in range(2)]
        w_dn = [W[i][:, 8 * D:12 * D].rearrange("p (k n) -> p k n", k=4) for i in range(2)]
        stage = [W[i // 3][:, i % 3 * 4 * D:(i % 3 + 1) * 4 * D] for i in range(6)]

        xT = sb("xT", [P, KD, NTOK])
        hT = sb("hT", [P, KD, NTOK])
        R1 = sb("R1", [P, 4 * D])
        rows = R1[:, :].rearrange("p (t d) -> p t d", t=4)
        oT = R1[:, :].rearrange("p (k t) -> p k t", k=KD)
        mixT = hT

        def part(region, lo, n, s=None, **kw):
            a = region[:, lo:lo + n]
            return a.rearrange(s, **kw) if s else a

        places = {}
        o = 0
        for name, n, s, kw in (("qa", 4 * NTOK, "p (h t) -> p h t", dict(h=4)), ("ka", 4 * NTOK, "p (h t) -> p h t", dict(h=4)),
                               ("bq", 2 * NTOK, "p (h t) -> p h t", dict(h=2)), ("bk", NTOK, None, {}),
                               ("dq", 4 * NTOK, "p (j v t) -> p j v t", dict(j=2, v=2)),
                               ("dk", 2 * NTOK, "p (h t) -> p h t", dict(h=2)), ("va", 4 * 256, "p (t c) -> p t c", dict(t=4)),
                               ("bv", 4 * P, "p (t c) -> p t c", dict(t=4)), ("dv", 4 * 256, "p (t c) -> p t c", dict(t=4)),
                               ("dg", 2 * NTOK, "p (j t) -> p j t", dict(j=2))):
            places[name] = [part(W[L % 2], o, n, s, **kw) for L in range(DEPTH)]
            o += n
        assert o <= EXP_W
        qas, kas, bqs, bks, dqs, dks, vas, bvs, dvs, dgs = places.values()
        prob = [part(R1, i * NTOK, NTOK) for i in range(3)] + [sb("prob3", [P, NTOK])]
        prob2 = part(R1, 3 * NTOK, NTOK)
        probT = [part(R1, (4 + i) * NTOK, NTOK, "p (k q) -> p k q", k=4) for i in range(2)]
        rope_c = [part(R1, 6 * NTOK + i * SEQ, SEQ) for i in range(2)]
        rope_s = [part(R1, 7 * NTOK + i * SEQ, SEQ) for i in range(2)]
        xg_in = [R1[0:BLK, i * D:(i + 1) * D] for i in range(2)]
        xg = R1[0:BLK, 2 * D:3 * D]
        xgT = part(R1, 3 * D, KD * BLK, "p (k s) -> p k s", k=KD)
        yb = rows
        x_tok = hT[:, 4:8, :].rearrange("p k t -> p (k t)").rearrange("p (t d) -> p t d", t=2)
        amp_row = xT[:, 0:2, :].rearrange("p k t -> p (k t)")

        lat = sb("lat", [P, 4 * NTOK])
        cq = part(lat, 0, 2 * NTOK, "p (j t) -> p j t", j=2)
        ckv = part(lat, 2 * NTOK, NTOK)
        kr = part(lat, 3 * NTOK, NTOK)
        ya = [hT[:, 2 * i:2 * i + 2, :].rearrange("p k t -> p (k t)") for i in range(2)] + [part(lat, i * D, D) for i in range(2)]
        w_dn_ahead = [[hT[:, 2 * k:2 * k + 2, :].rearrange("p k t -> p (k t)") for k in range(4)],
                      [xT[:, 2 * k + 2:2 * k + 4, :].rearrange("p k t -> p (k t)") for k in range(3)]
                      + [hT[:, 0:2, :].rearrange("p k t -> p (k t)")]]
        y_sb = [part(lat, i * 512, 512) for i in range(2)]
        silu_g, act_rows = (part(lat, 1024 + i * 256, 256) for i in range(2))
        actT = part(lat, 1536, 256, "p (c s) -> p c s", c=2)
        om = [part(lat, i * 4 * 256, 4 * 256, "p (q c) -> p q c", q=4) for i in range(2)]
        PADW = 288
        up = [sb(f"up{j}", [P, 2, PADW]) for j in range(2)]
        pa = sb("pa", [P, 2, PADW])
        pb = sb("pb", [P, 2, PADW])
        sq = [sb(f"sq{i}", [P, NTOK]) for i in range(2)]
        rstd = sb("rstd", [P, NTOK])
        cst = sb("cst", [P, CONSTANTS.shape[1]])
        ones = sb("ones", [P, P])
        band = sb("band", [P, 2 * SEQ], BF16)
        ident16 = sb("ident16", [P, P], BF16)
        w_uq = sb("w_uq", [P, 2, 384])
        w_ukv = sb("w_ukv", [P, 512])
        w_rt = sb("w_rt", [P, KD, 20])
        w_pool = sb("w_pool", [P, 2, P])
        vec_rows = sb("vec_rows", [P, P])
        bias_rows = sb("bias_rows", [P, P])
        vecT = sb("vecT", [P, 74])
        ada_bT = sb("ada_bT", [P, 96])
        c_sb = sb("c_sb", [P, 2, KD])
        c_t = sb("c_t", [P, 2, KD])
        silu_c = sb("silu_c", [P, KD, 32])
        ada_sb = sb("ada_sb", [P, 512])
        mod = [sb(f"mod{L}", [P, 48, 2]) for L in range(DEPTH)]
        amp = [sb(f"amp{L}", [P, 4, KD, 2]) for L in range(DEPTH)]
        rt_b = sb("rt_b", [P, DEPTH, 20])
        neg_sink = sb("neg_sink", [P, DEPTH * 4])
        dl = sb("dl", [P, DEPTH, 4, DIFF_QK])
        dlp = sb("dlp", [P, DEPTH, 2, DIFF_QK])
        dls = sb("dls", [P, DEPTH * 2])
        neg_lam = sb("neg_lam", [P, DEPTH])
        subln = sb("subln", [P, DEPTH, 64])
        st = sb("st", [P, 8, 8])
        dstat = sb("dstat", [P, 4, 16])
        lg = sb("lg", [P, 4, 20])
        rs = sb("rs", [P, 40, 4])
        r4 = sb("r4", [P, 10, 4, 4])
        r16 = sb("r16", [P, 6, 4, 16])
        cmp7 = sb("cmp7", [P, 16, 7])
        e16 = sb("e16", [P, 5, 16])
        spos = sb("spos", [P, 8], I32)
        spos_t = sb("spos_t", [P, 2, 8], I32)
        spos_f = sb("spos_f", [P, 2, 8])
        chosen = sb("chosen", [P, 5, 16])
        place_hot = part(lat, 0, 8 * BLK, "p (i s) -> p i s", i=8)
        block_id = part(lat, 8 * BLK, 8 * COLS, "p (i b) -> p i b", i=8)
        lgT = part(lat, 2 * NTOK, NTOK)
        zeros = sb("zeros", [P, D // 2])
        slots = sb("slots", [BLK, COLS], I32)
        slot_col = sb("slot_col", [BLK, 2], I32)
        tabs = [sb(f"tab{L}", [P, 64], I32) for L in range(DEPTH)]
        T_NB, T_START, T_CUM, T_TOTAL = 0, 16, 32, 48

        psum = ctx.enter_context(nc.psum_tensor("psum", [P, 8, 512], F32))
        RING, B_SUM, B_ADA = range(6), 6, 7

        def C(name, rows_=P):
            a, b = CST[name]
            return cst[0:rows_, a:b]

        ident = C("ident")
        inv_count = C("inv_count").rearrange("p (j t) -> p j t", j=2)

        def gain(L, i, k):
            return vecT[:, L * 32 + i * 8 + k:L * 32 + i * 8 + k + 1]

        def q_tokens(L):
            return NTOK if L == 0 else SEQ

        def streams(lo, hi):
            return [(s, s * SEQ, (s + 1) * SEQ) for s in range(lo // SEQ, hi // SEQ)]

        def spans(L, w):
            return [(0, NTOK)] if (L, w) == (0, 1) else streams_of(NTOK if w == 1 else q_tokens(L))

        def streams_of(n):
            return [(lo, lo + SEQ) for lo in range(0, n, SEQ)]

        def out_plan(L):
            plan = [("some", (0, SEQ), m) for m in range(N_SOME)] + [("merge", (0, SEQ))]
            for n, span in enumerate(streams_of(q_tokens(L))):
                before = {3: [("norm", plan_span)], 5: [("h", plan_span)], 6: [("logits", plan_span)]} if n else {}
                for m in range(KD):
                    plan += before.get(m, [])
                    plan.append(("out", span, m))
                    if m:
                        plan.append(("sum", span, m - 1))
                plan += [("sum", span, KD - 1), ("add", span)]
                plan_span = span
            return plan + [("norm", plan_span), ("h", plan_span), ("logits", plan_span)]

        N_SOME = 4
        K_SOME, K_DIFF = (0, 1, 2, 3, 6, 7), (4, 5)

        AHEAD = 3

        ROPED_LATE = {3: "dq0", 4: "dk0", 5: "dq1", 6: "dk1"}

        KINDS = ("mla", "swa", "diff")

        def units(L):
            return [(kind, qt, h) for kind in KINDS for qt in range(q_tokens(L) // P) for h in range(HEADS)]

        TILES = {"cq0": (0, 0), "cq1": (P, 0), "ckv": (C_CKV, 1), "kr": (C_KR, 1), "bk": (C_BK - C_BQ, 1), "bq0": (0, 0),
                 "bq1": (0, 0), "dq0": (0, 0), "dq1": (P, 0), "dk0": (C_DK - C_DQ, 1), "dk1": (C_DK - C_DQ + P, 1),
                 "u0": (C_U - C_DV, 0), "u1": (C_U - C_DV + P, 0)}
        VALUES = {"bv": (P, range(4)), "dv0": (256, range(2)), "dv1": (256, range(2, 4))}
        ROPES = [{"kr": (kr[64:96, 0:SEQ], "mla", 64, 96), "bk": (bks[L][:, 0:SEQ], "swa", 0, P)} for L in range(DEPTH)]
        for L in range(DEPTH):
            for j in range(2):
                ROPES[L][f"bq{j}"] = (bqs[L][:, j, 0:SEQ], "swa", 0, P)
                ROPES[L][f"dq{j}"] = (dqs[L][:, j, 0, 0:SEQ], "diff", 0, P)
                ROPES[L][f"dk{j}"] = (dks[L][:, j, 0:SEQ], "diff", 0, P)
            for i in range(HEADS):
                ROPES[L][f"qa{i}"] = (qas[L][0:MLA_QK, i, 0:SEQ], "mla", 0, MLA_QK)

        items = [("ada", 0, i) for i in range(4)] + [("in", 0, i) for i in range(3)]
        items += [("ada", 0, 4), ("in", 0, 3)] + [("ada", 0, i) for i in range(5, 12)] + [("ada", 1, i) for i in range(12)]
        items += [("out", 0, i) for i in range(2)]
        n_stage0 = len(items)
        items += [("in", 1, i) for i in range(4)] + [("out", 1, i) for i in range(2)]
        item_no = {it: n for n, it in enumerate(items)}
        first_buffers = {("ada", 0, 0): 0, ("ada", 0, 1): 1, ("ada", 0, 2): 2, ("ada", 0, 3): 5}
        buffers, n = [], 0
        for it in items[:n_stage0]:
            if it[:2] == ("ada", 0) and it[2] < 7:
                buffers.append(first_buffers.get(it, 0))
            else:
                buffers.append(3 + n % 3)
                n += 1
        buffers += [n % 3 for n in range(len(items) - n_stage0)]

        def stage_source(it):
            kind, L, i = it
            if kind == "ada":
                r, kk = i // 4, i % 4
                return A["ada_w"][L].rearrange("(p k) n -> p k n", k=KD)[:, 2 * kk:2 * kk + 2, r * 2048:(r + 1) * 2048]
            if kind == "in":
                a, b = IN_CHUNKS[i]
                return A["w_in"][L].rearrange("(k p) n -> p k n", p=P)[:, :, a:b]
            return A["w_out"][L].rearrange("(k p) n -> p k n", p=P)[:, :, i * 512:(i + 1) * 512]

        def staged(it):
            kind, L, i = it
            b = stage[buffers[item_no[it]]]
            if kind == "ada":
                return b.rearrange("p (k g n) -> p k g n", k=2, g=4)
            n = IN_CHUNKS[i][1] - IN_CHUNKS[i][0] if kind == "in" else 512
            return b[:, 0:KD * n].rearrange("p (k n) -> p k n", k=KD)

        def ada_plan(L):
            return [it for it in items if it[0] == "ada" and it[1:] >= (0, 7)] if L == 0 else []

        block = ctx.enter_context(nc.Block())

        @block.tensor
        def _(pe):
            last_read = {}
            taken = {}

            def reuse(bank, key):
                if bank in last_read:
                    pe.wait_ge(*at(*last_read[bank]))
                last_read[bank] = key
                taken[bank] = len(M.where) + len(taken) / 10

            def take(*job, banks=RING):
                bank = min(banks, key=lambda x: taken.get(x, -1))
                reuse(bank, ("read",) + job)
                M.bank_of[job] = bank
                return psum[:, bank, :]

            def square_part(S, tag, k, count, src):
                bank = B_ADA if tag[:2] in ((0, 2), (1, 2)) else B_SUM
                if k == 0:
                    reuse(bank, ("sum_read", tag))
                pe.wait_ge(*at("sq", tag, k))
                nc.tensor.matmul(psum[:, bank, 0:src.shape[1]], ones[:, :], src, start=(k == 0), stop=(k == count - 1))\
                    .then_inc(*mark(S, ("sq_used", tag, k)))

            def ada_item(S, it):
                _, L, i = it
                pe.wait_ge(*at("staged", item_no[it]))
                r, kk = i // 4, i % 4
                if kk == 0:
                    reuse(B_ADA, ("ada_sb", L, r))
                w = staged(it)
                for k2 in range(2):
                    k = 2 * kk + k2
                    for g in range(4):
                        mm = nc.tensor.matmul(psum[32 * g:32 * g + 32, B_ADA, :], silu_c[:, k, :], w[:, k2, g, :],
                                              start=(k == 0), stop=(k == 7), skip_group_check=True)
                mm.then_inc(*mark(S, ("used", item_no[it])))

            def ada_turn(S, L, r):
                pe.wait_ge(*at("ada_sb", L, r))
                t = take("adaT", L, r)
                for q in range(4):
                    mm = nc.tensor.transpose(t[:, q * P:(q + 1) * P], ada_sb[:, q * P:(q + 1) * P], ident)
                mm.then_inc(*mark(S, ("filled", "adaT", L, r)))

            def norm(S, L, w, span):
                for k in range(KD):
                    square_part(S, (L, w, span), k, KD, sq[k % 2][:, 0:span[1] - span[0]])

            def project(L):
                S, nq = f"pe_in{L}", q_tokens(L)

                def tile(name, w, t, lo, hi):
                    col, _ = TILES[name]
                    m, p0 = (MLA_ROPE, MLA_NOPE) if name == "kr" else (P, 0)
                    for k in range(KD):
                        if name in ("cq0", "ckv"):
                            span = [s for s in spans(L, 1) if s[0] <= lo < s[1]][0]
                            pe.wait_ge(*at("h", L, 1, span, k))
                        if name in ("bq0", "bq1"):
                            for b in range(2):
                                c0 = b * P + int(name[2]) * 64
                                mm = nc.tensor.matmul(t[64 * b:64 * b + 64, lo:hi], w[:, k, c0:c0 + 64], hT[:, k, lo:hi],
                                                      start=(k == 0), stop=(k == KD - 1), skip_group_check=True)
                        else:
                            mm = nc.tensor.matmul(t[p0:p0 + m, lo:hi], w[:, k, col:col + m], hT[:, k, lo:hi],
                                                  start=(k == 0), stop=(k == KD - 1))
                    return mm

                for c, names in enumerate((("cq0", "cq1", "ckv", "kr"), ("bk", "bv", "bq0", "bq1"),
                                           ("dq0", "dk0", "dq1", "dk1"), ("dv0", "dv1", "u0", "u1"))):
                    it = ("in", L, c)
                    pe.wait_ge(*at("staged", item_no[it]))
                    w = staged(it)
                    if c == 0 and L:
                        for name in ("cq0", "cq1"):
                            tile(name, w, take(name, L), 0, SEQ).then_inc(*mark(S, ("filled", name, L)))
                        norm(S, L, 1, (SEQ, NTOK))
                        t = {name: take(name, L) for name in ("ckv", "kr")}
                        for lo in (0, SEQ):
                            for name in ("ckv", "kr"):
                                mm = tile(name, w, t[name], lo, lo + SEQ)
                                if lo:
                                    used = [("used", item_no[it])] if name == "kr" else []
                                    mm.then_inc(*mark(S, ("filled", name, L), *used))
                        continue
                    for name in names:
                        t = take(name, L)
                        if name in VALUES:
                            width, tts = VALUES[name]
                            col = (C_BV - C_BQ) if name == "bv" else 0
                            for i, tt in enumerate(tts):
                                for k in range(KD):
                                    mm = nc.tensor.matmul(t[:, i * width:(i + 1) * width], hT[:, k, tt * P:(tt + 1) * P],
                                                          w[:, k, col:col + width], start=(k == 0), stop=(k == KD - 1))
                        else:
                            mm = tile(name, w, t, 0, NTOK if TILES[name][1] else nq)
                        used = [("used", item_no[it])] if name == names[-1] else []
                        mm.then_inc(*mark(S, ("filled", name, L), *used))
                        if used and L == 0 and c:
                            ada_item(S + "_ada", ("ada", 0, 3 + c))
                        if name == "bk":
                            for j in range(2):
                                square_part(S, ("cq", L), j, 2, sq[j][:, 0:nq])
                        if name == "bq1":
                            square_part(S, ("ckv", L), 0, 1, sq[0][:, :])

            def rotate(S, L, name, x, kind, lo, hi):
                pe.wait_ge(*at("tile", L, name))
                t = take("rot", L, name)
                r = C("rot_" + kind)
                nc.tensor.matmul(t[lo:hi, 0:SEQ], r[lo:hi, lo:hi], x, start=True, stop=True)\
                    .then_inc(*mark(S, ("filled", "rot", L, name)))

            def latent_projections(L):
                S, nq = f"pe_lat{L}", q_tokens(L)
                pe.wait_ge(*at("const"))
                for name in ("kr", "bk", "bq0", "bq1"):
                    x, kind, lo, hi = ROPES[L][name]
                    rotate(S, L, name, x, kind, lo, hi)
                pe.wait_ge(*at("small_w", L))
                pe.wait_ge(*at("cqn", L))
                for h in range(HEADS):
                    t = take("qa", L, h)
                    for j in range(2):
                        mm = nc.tensor.matmul(t[0:MLA_QK, 0:nq], w_uq[:, j, h * MLA_QK:(h + 1) * MLA_QK], cq[:, j, 0:nq],
                                              start=(j == 0), stop=(j == 1))
                    mm.then_inc(*mark(S, ("filled", "qa", L, h)))
                pe.wait_ge(*at("ckvn", L))
                for h in range(HEADS):
                    t = take("ka", L, h)
                    nc.tensor.matmul(t[0:MLA_NOPE, :], w_ukv[:, h * P:h * P + MLA_NOPE], ckv, start=True, stop=True)\
                        .then_inc(*mark(S, ("filled", "ka", L, h)))
                wv = w_ukv[:, :].rearrange("p (h c) -> p h c", h=HEADS)[:, :, MLA_NOPE:P]
                for j in range(2):
                    t = take("va", L, j)
                    for i in range(2):
                        tt = 2 * j + i
                        mm = nc.tensor.matmul(t[:, i * 256:(i + 1) * 256], ckv[:, tt * P:(tt + 1) * P], wv,
                                              start=True, stop=True)
                    mm.then_inc(*mark(S, ("filled", "va", L, j)))
                for name in ("qa0", "qa1", "qa2", "qa3"):
                    x, kind, lo, hi = ROPES[L][name]
                    rotate(S, L, name, x, kind, lo, hi)

            def mix(L):
                S = f"pe_mix{L}"
                U, nq = units(L), q_tokens(L)
                ada, done = ada_plan(L), 0
                ring = range(B_ADA if L == 0 else 8)

                def scores(u):
                    kind, qt, h = U[u]
                    nk = NTOK if qt < 2 else SEQ
                    keys, qs = slice(NTOK - nk, NTOK), slice(qt * P, (qt + 1) * P)
                    if kind == "mla":
                        if qt == 0:
                            pe.wait_ge(*at("roped", L, f"qa{h}"))
                            pe.wait_ge(*at("ka", L, h))
                            pe.wait_ge(*at("kr_out", L, h))
                        t = take("s", L, u, 0, banks=ring)
                        nc.tensor.matmul(t[:, 0:nk], qas[L][0:MLA_QK, h, qs], kas[L][0:MLA_QK, h, keys], start=True, stop=True)\
                            .then_inc(*mark(S, ("filled", "s", L, u, 0)))
                    elif kind == "swa":
                        if qt == 0 and h == 0:
                            pe.wait_ge(*at("roped", L, "bq1"))
                        t = take("s", L, u, 0, banks=ring)
                        lo, local = 64 * (h // 2), qt < 2
                        if local:
                            nc.tensor.matmul(t[:, 0:SEQ], bqs[L][lo:lo + 64, h % 2, qs], bks[L][lo:lo + 64, 0:SEQ], start=True, stop=False)
                            nc.tensor.matmul(t[:, 0:SEQ], ident16[:, :], band[:, qt * SEQ:(qt + 1) * SEQ], start=False, stop=True)
                        mm = nc.tensor.matmul(t[:, nk - SEQ:nk], bqs[L][lo:lo + 64, h % 2, qs], bks[L][lo:lo + 64, SEQ:NTOK],
                                              start=True, stop=True)
                        mm.then_inc(*mark(S, ("filled", "s", L, u, 0)))
                    else:
                        if qt == 0 and h == 0:
                            pe.wait_ge(*at("dq_split", L, 1))
                            pe.wait_ge(*at("roped", L, "dk1"))
                        j, lo = h // 2, 64 * (h % 2)
                        for v in range(2):
                            t = take("s", L, u, v, banks=ring)
                            nc.tensor.matmul(t[:, 0:nk], dqs[L][lo:lo + 64, j, v, qs], dks[L][lo:lo + 64, j, keys],
                                             start=True, stop=True).then_inc(*mark(S, ("filled", "s", L, u, v)))

                def turn(u):
                    kind, qt, h = U[u]
                    pe.wait_ge(*at("prob", L, u))
                    t = take("pT", L, u, banks=ring)
                    for i in range(4 if qt < 2 else 2):
                        mm = nc.tensor.transpose(t[:, i * P:(i + 1) * P], prob[u % (AHEAD + 1)][:, i * P:(i + 1) * P], ident)
                    mm.then_inc(*mark(S, ("filled", "pT", L, u)))

                def values(u):
                    kind, qt, h = U[u]
                    n, k0 = (4, 0) if qt < 2 else (2, 2)
                    pe.wait_ge(*at("probT", L, u))
                    if qt == 0 and h == 0:
                        pe.wait_ge(*at("v", L, kind))
                    t = take("o", L, u, banks=ring)
                    for i in range(n):
                        v = {"mla": vas[L][:, k0 + i, h * 64:h * 64 + 64], "diff": dvs[L][:, k0 + i, h * 64:h * 64 + 64],
                             "swa": bvs[L][:, k0 + i, (h // 2) * 64:(h // 2) * 64 + 64]}[kind]
                        mm = nc.tensor.matmul(t[:, 0:64], probT[u % 2][:, i, :], v, start=(i == 0), stop=(i == n - 1))
                    mm.then_inc(*mark(S, ("filled", "o", L, u)))

                def merge(kind):
                    pe.wait_ge(*at("om", L, kind))
                    for j in range(2):
                        t = take("mT", L, kind, j, banks=ring)
                        for qt in range(nq // P):
                            mm = nc.tensor.transpose(t[:, qt * P:(qt + 1) * P],
                                                     om[KINDS.index(kind) % 2][:, qt, j * P:(j + 1) * P], ident)
                        mm.then_inc(*mark(S, ("filled", "mT", L, kind, j)))

                per = len(U) // 3
                for i in range(len(U) + AHEAD + 1):
                    if i < len(U):
                        scores(i)
                    if AHEAD <= i < len(U) + AHEAD:
                        turn(i - AHEAD)
                    if i > AHEAD:
                        values(i - AHEAD - 1)
                    if i in ROPED_LATE:
                        x, kind, lo, hi = ROPES[L][ROPED_LATE[i]]
                        rotate(S, L, ROPED_LATE[i], x, kind, lo, hi)
                    if i in (per + AHEAD + 4, 2 * per + AHEAD + 4):
                        merge(KINDS[(i - AHEAD - 4) // per - 1])
                    if i == 2 * per + AHEAD + 7:
                        for j in range(2):
                            pe.wait_ge(*at("dg", L, j))
                            t = take("pool", L, j, banks=ring)
                            nc.tensor.matmul(t[:, 0:nq], w_pool[:, j, :], dgs[L][:, j, 0:nq], start=True, stop=True)\
                                .then_inc(*mark(S, ("filled", "pool", L, j)))
                    while done < len(ada) and done * len(U) <= i * len(ada):
                        ada_item(S, ada[done])
                        _, la, ia = ada[done]
                        done += 1
                        if ia % 4 == 1 and (la, ia) != (0, 5):
                            ada_turn(S, *((la, ia // 4 - 1) if ia // 4 else (la - 1, 2)))
                if ada:
                    ada_turn(S, 1, 2)
                return merge

            def project_out(L, merge):
                S, n = f"pe_out{L}", SEQ
                pe.wait_ge(*at("mixT_some", L))
                begun = {}
                for what, span, *rest in out_plan(L):
                    lo, hi = span
                    if what == "some":
                        m, = rest
                        pe.wait_ge(*at("staged", item_no[("out", L, 0)]))
                        w = staged(("out", L, 0))
                        t = begun[m] = take("oT", L, lo, m)
                        for k in K_SOME:
                            nc.tensor.matmul(t[:, 0:n], w[:, k, m * P:(m + 1) * P], mixT[:, k, lo:hi], start=(k == 0), stop=False)
                    elif what == "merge":
                        merge("diff")
                        pe.wait_ge(*at("mixT", L))
                    elif what == "out":
                        m, = rest
                        it = ("out", L, m // 4)
                        if m % 4 == 0:
                            pe.wait_ge(*at("staged", item_no[it]))
                        w = staged(it)
                        ks = K_DIFF if lo == 0 and m in begun else K_SOME + K_DIFF
                        t = begun[m] if ks == K_DIFF else take("oT", L, lo, m)
                        for k in ks:
                            mm = nc.tensor.matmul(t[:, 0:n], w[:, k, (m % 4) * P:(m % 4 + 1) * P], mixT[:, k, lo:hi],
                                                  start=(k == 0), stop=(k == ks[-1]))
                        used = [("used", item_no[it])] if m % 4 == 3 and hi == q_tokens(L) else []
                        mm.then_inc(*mark(S, ("filled", "oT", L, lo, m), *used))
                    elif what == "sum":
                        m, = rest
                        square_part(S, ("o", L, span), m, KD, sq[m % 2][:, 0:n])
                    elif what == "norm":
                        norm(S, L, 2, span)
                    elif what == "logits":
                        pe.wait_ge(*at("small_w", L))
                        t = take("lgT", L, lo)
                        for k in range(KD):
                            pe.wait_ge(*at("h", L, 2, span, k))
                            mm = nc.tensor.matmul(t[0:20, 0:n], w_rt[:, k, :], hT[:, k, lo:hi], start=(k == 0), stop=(k == KD - 1))
                        mm.then_inc(*mark(S, ("filled", "lgT", L, lo)))

            def route(L):
                S, nt = f"pe_route{L}", q_tokens(L) // P
                pe.wait_ge(*at("lgT", L))
                t = take("lg", L)
                for tt in range(nt):
                    mm = nc.tensor.transpose(t[:, tt * 20:tt * 20 + 20], lgT[0:20, tt * P:(tt + 1) * P], ident[0:20, 0:20])
                mm.then_inc(*mark(S, ("filled", "lg", L)))
                for tt in range(nt):
                    for half in range(2):
                        t = take("hr", L, tt, half)
                        for i in range(4):
                            mm = nc.tensor.transpose(t[:, i * P:(i + 1) * P], hT[:, 4 * half + i, tt * P:(tt + 1) * P], ident)
                        mm.then_inc(*mark(S, ("filled", "hr", L, tt, half)))
                if L == DEPTH - 1:
                    for tt in range(nt):
                        for half in range(2):
                            t = take("xr", tt, half)
                            for i in range(4):
                                mm = nc.tensor.transpose(t[:, i * P:(i + 1) * P], xT[:, 4 * half + i, tt * P:(tt + 1) * P], ident)
                            mm.then_inc(*mark(S, ("filled", "xr", tt, half)))
                pe.wait_ge(*at("chosen", L))
                t = take("rk", L)
                nc.tensor.matmul(t[:, 0:(nt + 1) * 16], C("before"), chosen[:, 4 - nt:5, :], start=True, stop=False)
                for i in range(nt):
                    mm = nc.tensor.matmul(t[:, (i + 1) * 16:(nt + 1) * 16], ones[:, :],
                                          chosen[:, 4 - nt + i, :].unsqueeze(1).to_broadcast([P, nt - i, 16]),
                                          start=False, stop=(i == nt - 1))
                mm.then_inc(*mark(S, ("filled", "rk", L)))
                pe.wait_ge(*at("slot_hot", L))
                t = take("st", L)
                for i in range(2 * nt):
                    mm = nc.tensor.matmul(t[0:BLK, 0:COLS], place_hot[:, i, :], block_id[:, i, :], start=(i == 0), stop=(i == 2 * nt - 1))
                mm.then_inc(*mark(S, ("filled", "st", L)))
                if L == DEPTH - 1:
                    for half in range(2):
                        pe.wait_ge(*at("diagonal", half))
                        t = take("amp_row", half)
                        nc.tensor.matmul(t, ones[:, :], sq[half][:, :], start=True, stop=True)\
                            .then_inc(*mark(S, ("filled", "amp_row", half)))

            def experts(L):
                for bank in range(4):
                    pe.wait_ge(*at(*last_read[bank]))
                xt_ps, gu_ps, at_ps, y_ps = (psum[:, b, :] for b in range(4))
                x_rows, x_turned, x_ready = sem(f"x_rows{L}"), sem(f"x_turned{L}"), sem(f"x_ready{L}")
                gu_done, act_ready = sem(f"gu_done{L}"), sem(f"act_ready{L}")
                act_turned, actT_ready, y_done = sem(f"act_turned{L}"), sem(f"actT_ready{L}"), sem(f"y_done{L}")

                def turn_x(g):
                    pe.wait_ge(x_rows, g + 1)
                    pe.sem_inc(sem("pe_hold"), 1)
                    for k in range(KD):
                        mm = nc.tensor.transpose(xt_ps[:, k * BLK:(k + 1) * BLK], xg[:, k * P:(k + 1) * P], ident[0:BLK, 0:BLK])
                    mm.then_inc(x_turned, 1)

                def gate_up(g, place, landed=None):
                    pe.wait_ge(x_ready, g + 1)
                    for k in range(KD):
                        if landed is not None and k % 4 == 0:
                            pe.wait_ge(sem(f"w_{('lo', 'hi')[k // 4]}{place}"), landed)
                            pe.sem_inc(sem("pe_hold"), 1)
                        for j in range(2):
                            mm = nc.tensor.matmul(gu_ps[64 * j:64 * j + 64, :], xgT[:, k, :], w_gu[place][:, k, j, :, :],
                                                  start=(k == 0), stop=(k == KD - 1), skip_group_check=True)
                        if k == KD // 2 - 1:
                            mm.then_inc(sem(f"lo_done{L}"), 1)
                    mm.then_inc(gu_done, 1)

                def turn_act(g):
                    pe.wait_ge(act_ready, g + 1)
                    for c in range(2):
                        mm = nc.tensor.transpose(at_ps[:, c * P:(c + 1) * P], act_rows[:, c * P:(c + 1) * P], ident)
                    mm.then_inc(act_turned, 1)

                def down(g, w):
                    pe.wait_ge(actT_ready, g + 1)
                    for kk in range(4):
                        for j in range(2):
                            mm = nc.tensor.matmul(y_ps[64 * j:64 * j + 64, :],
                                                  actT[:, kk % 2, (kk // 2) * 64:(kk // 2) * 64 + 64],
                                                  w[kk][:, j * 512:(j + 1) * 512],
                                                  start=(kk == 0), stop=(kk == 3), skip_group_check=True)
                    mm.then_inc(y_done, 1)

                turn_x(0)
                pe.wait_ge(*at("tab", L))
                down_of = [[w_dn[p][:, kk, :] for kk in range(4)] for p in range(2)]

                def expert(pair, par, w, w_last):
                    place = (par + L) % 2
                    n_blocks = pe.value_load(tabs[L][0:1, ds(pair * 2 + (T_NB + par), 1)], min_val=1, max_val=8)
                    start = pe.value_load(tabs[L][0:1, ds(pair * 2 + (T_START + par), 1)], min_val=0, max_val=MAXBLK)
                    landed = (pair + (L * (N_EXP // 2) + 1)) * 16
                    gate_up(start, place, landed)
                    turn_x(start + 1)
                    if w_last is not None:
                        down(start - 1, w_last)
                    turn_act(start)
                    if w is w_dn_ahead[L]:
                        pe.wait_ge(*at("ahead", L))
                    else:
                        before = L * (N_EXP // 2 - (1 if par else 0))
                        own = pair if par == 0 and not (isinstance(pair, int) and pair == 0) else pair + 1
                        pe.wait_ge(sem(f"w_dn{place}"), (own + before) * 16)
                    pe.sem_inc(sem("pe_hold"), 1)
                    with pe.If(n_blocks > 1):
                        with pe.Fori(start + 1, start + n_blocks) as g:
                            gate_up(g, place)
                            turn_x(g + 1)
                            down(g - 1, w)
                            turn_act(g)

                even, odd = down_of[L % 2], down_of[1 - L % 2]
                expert(0, 0, even, None)
                expert(0, 1, odd, even)
                expert(1, 0, w_dn_ahead[L], odd)
                expert(1, 1, odd, w_dn_ahead[L])
                with pe.Fori(2, N_EXP // 2) as pair:
                    expert(pair, 0, even, odd)
                    expert(pair, 1, odd, even)
                total = pe.value_load(tabs[L][0:1, T_TOTAL:T_TOTAL + 1], min_val=N_EXP, max_val=MAXBLK)
                down(total - 1, odd)
                pe.wait_ge(y_done, total)
                pe.wait_ge(x_ready, total + 1)
                for s in (gu_done, x_turned, act_turned):
                    pe.sem_inc(s, 1)

            def turn_combined(S, L, span):
                lo, hi = span
                for tt in range(lo // P, hi // P):
                    pe.wait_ge(*at("y_norm", L, tt))
                for kk in range(KD // 2):
                    t = take("yT", L, lo, kk)
                    for i in range(2):
                        for tt in range(2):
                            mm = nc.tensor.transpose(t[:, (2 * i + tt) * P:(2 * i + tt + 1) * P],
                                                     ya[lo // P + tt][:, (2 * kk + i) * P:(2 * kk + i + 1) * P], ident)
                    mm.then_inc(*mark(S, ("filled", "yT", L, lo, kk)))

            S0 = "pe_start"
            for key in (("soon",), ("ones",), ("vec_rows",)):
                pe.wait_ge(*at(*key))
            t = take("vec")
            nc.tensor.transpose(t[:, 0:74], vec_rows[0:74, :], ident[0:74, 0:74])
            nc.tensor.transpose(t[:, P:P + 96], bias_rows[0:96, :], ident[0:96, 0:96])\
                .then_inc(*mark(S0, ("filled", "vec")))
            pe.wait_ge(*at("x_rows"))
            for k in range(KD):
                t = take("x0", k)
                for tt in range(4):
                    mm = nc.tensor.transpose(t[:, tt * P:(tt + 1) * P], rows[:, tt, k * P:(k + 1) * P], ident)
                mm.then_inc(*mark(S0, ("filled", "x0", k)))
            pe.wait_ge(*at("silu_c"))
            ada_item(S0 + "_ada0", ("ada", 0, 0))
            norm(S0 + "_norm", 0, 1, (0, NTOK))
            for i in range(1, 4):
                ada_item(S0 + "_ada", ("ada", 0, i))
            ada_turn(S0 + "_turn", 0, 0)
            for L in range(DEPTH):
                if L:
                    pe.wait_ge(*at("banks_out", L - 1))
                    turn_combined("pe_comb", L - 1, (0, SEQ))
                    norm("pe_norm", L, 1, (0, SEQ))
                    turn_combined("pe_comb1", L - 1, (SEQ, NTOK))
                project(L)
                latent_projections(L)
                merge = mix(L)
                project_out(L, merge)
                route(L)
                experts(L)

        def read(eng, *job):
            eng.wait_ge(*at("filled", *job))
            return psum[:, M.bank(*job), :]

        @block.scalar
        def _(act):
            a = nc.scalar.activation
            squared = {}

            def square(S, tag, k, src, n, buf):
                if buf in squared:
                    act.wait_ge(*at("sq_used", *squared[buf]))
                squared[buf] = (tag, k)
                a(sq[buf][:, 0:n], src, ACT.Square).then_inc(*mark(S, ("sq", tag, k)))

            def finish_rstd(S, tag, last, span, width, free, bank=B_SUM):
                lo, hi = span
                act.wait_ge(*at("sq_used", tag, last))
                if free:
                    act.wait_ge(*at(*free))
                a(rstd[:, lo:hi], psum[:, bank, 0:hi - lo], ACT.Ln, scale=1.0 / width, bias=C("eps"))\
                    .then_inc(*mark(S, ("sum_read", tag)))
                act.wait_ge(*at("sum_read", tag))
                a(rstd[:, lo:hi], rstd[:, lo:hi], ACT.Exp, scale=-0.5).then_inc(*mark(S, ("rstd", tag)))

            def norm(L, w, span, free):
                S, n = f"act_norm{w}{L}{span[0]}", span[1] - span[0]
                for k in range(KD):
                    if L == 0 and w == 1:
                        act.wait_ge(*at("read", "x0", k))
                    elif w == 1:
                        act.wait_ge(*at("x", L - 1, 2, span, k))
                    else:
                        act.wait_ge(*at("x", L, 1, span, k))
                    square(S, (L, w, span), k, xT[:, k, span[0]:span[1]], n, k % 2)
                finish_rstd(S, (L, w, span), KD - 1, span, D, free, B_ADA if w == 2 else B_SUM)

            def modulate(L, w, span):
                S = f"act_mod{w}{L}{span[0]}"
                act.wait_ge(*at("amp", L, 0 if w == 1 else 2))
                b0 = 0 if w == 1 else 24
                for k in range(KD):
                    act.wait_ge(*at("xn", L, w, span, k))
                    for s, lo, hi in streams(*span):
                        ins = a(hT[:, k, lo:hi], hT[:, k, lo:hi], ACT.Identity,
                                scale=amp[L][:, 0 if w == 1 else 2, k, s:s + 1], bias=mod[L][:, b0 + k, s:s + 1])
                    ins.then_inc(*mark(S, ("h", L, w, span, k)))

            def copy(S, dst, job, n=NTOK, lo=0, hi=P, scale=1.0, keys=()):
                src = read(act, *job)[lo:hi, 0:n]
                a(dst, src, ACT.Copy, scale=scale).then_inc(*mark(S, ("read", *job), *keys))

            def project(L):
                S, nq = f"act_in{L}", q_tokens(L)
                for j in range(2):
                    copy(S, cq[:, j, 0:nq], (f"cq{j}", L), nq)
                for j in range(2):
                    act.wait_ge(*at("read", f"cq{j}", L))
                    square(S, ("cq", L), j, cq[:, j, 0:nq], nq, j)
                copy(S, ckv, ("ckv", L))
                copy(S, kr[64:96, :], ("kr", L), lo=64, hi=96, keys=[("tile", L, "kr")])
                copy(S, bks[L], ("bk", L), keys=[("tile", L, "bk")])
                finish_rstd(S, ("cq", L), 1, (0, nq), 256, ("xn", L, 1, spans(L, 1)[-1], KD - 1))
                square(S, ("ckv", L), 0, ckv, NTOK, 0)
                copy(S, bvs[L][:, :, :].rearrange("p t c -> p (t c)"), ("bv", L), keys=[("v", L, "swa")])
                for j in range(2):
                    copy(S, bqs[L][:, j, 0:nq], (f"bq{j}", L), nq, scale=SWA_SCALE, keys=[("tile", L, f"bq{j}")])
                finish_rstd(S, ("ckv", L), 0, (0, NTOK), 128, ("cqn", L))
                for j in range(2):
                    copy(S, dqs[L][:, j, 0, 0:nq], (f"dq{j}", L), nq, scale=DIFF_SCALE, keys=[("tile", L, f"dq{j}")])
                    copy(S, dks[L][:, j, :], (f"dk{j}", L), keys=[("tile", L, f"dk{j}")])
                for j in range(2):
                    copy(S, dvs[L][:, 2 * j:2 * j + 2, :].rearrange("p t c -> p (t c)"), (f"dv{j}", L),
                         keys=[("v", L, "diff")] if j else [])
                for j in range(2):
                    if L == 0:
                        act.wait_ge(*at("pads"))
                    else:
                        act.wait_ge(*at("dg", L - 1, j))
                    src = read(act, f"u{j}", L)
                    ns = nq // SEQ
                    a(up[j][:, 0:ns, 16:16 + SEQ], src[:, 0:nq].rearrange("p (s t) -> p s t", s=ns), ACT.Copy)\
                        .then_inc(*mark(S, ("read", f"u{j}", L)))

            def latent_projections(L):
                S, nq = f"act_lat{L}", q_tokens(L)
                for h in range(HEADS):
                    copy(S, qas[L][0:MLA_QK, h, 0:nq], ("qa", L, h), nq, hi=MLA_QK, scale=MLA_SCALE, keys=[("tile", L, f"qa{h}")])
                for h in range(HEADS):
                    copy(S, kas[L][0:MLA_NOPE, h, :], ("ka", L, h), hi=MLA_NOPE, keys=[("ka", L, h)])
                for j in range(2):
                    copy(S, vas[L][:, 2 * j:2 * j + 2, :].rearrange("p t c -> p (t c)"), ("va", L, j),
                         keys=[("v", L, "mla")] if j else [])

            def mix(L):
                S = f"act_mix{L}"
                U, nq = units(L), q_tokens(L)
                per = len(U) // 3

                def softmax(u):
                    kind, qt, h = U[u]
                    nk = NTOK if qt < 2 else SEQ
                    act.wait_ge(*at("nmax", L, u))
                    if u > AHEAD:
                        act.wait_ge(*at("filled", "pT", L, u - AHEAD - 1))
                    if u >= 8:
                        act.wait_ge(*at("read", "o", L, u - 8))
                    s_ = st[:, u % 8, :]
                    for v in range(2 if kind == "diff" else 1):
                        if v == 1 and U[u - 1][0] == "diff":
                            act.wait_ge(*at("prob", L, u - 1))
                        a((prob[u % (AHEAD + 1)] if v == 0 else prob2)[:, 0:nk], read(act, "s", L, u, v)[:, 0:nk], ACT.Exp,
                          bias=s_[:, v:v + 1], accum_out=s_[:, 2 + v:3 + v])\
                            .then_inc(*mark(S, ("read", "s", L, u, v), *([("prob", L, u)] if kind != "diff" else [])))
                    if kind == "swa":
                        a(s_[:, 4:5], neg_sink[:, L * 4 + h:L * 4 + h + 1], ACT.Exp, scale=-1.0, bias=s_[:, 0:1])\
                            .then_inc(*mark(S, ("sink", L, u)))

                def probs_out(u):
                    kind, qt, h = U[u]
                    n = 4 if qt < 2 else 2
                    src = read(act, "pT", L, u)
                    if u >= 2:
                        act.wait_ge(*at("filled", "o", L, u - 2))
                    a(probT[u % 2][:, 0:n, :], src[:, 0:n * P].rearrange("p (k q) -> p k q", k=n), ACT.Copy)\
                        .then_inc(*mark(S, ("read", "pT", L, u), ("probT", L, u)))

                def merge(kind):
                    for j in range(2):
                        copy(S, mixT[:, 2 * KINDS.index(kind) + j, 0:nq], ("mT", L, kind, j), nq,
                             keys=[("mixT", L)] if kind == "diff" and j else [])

                for i in range(len(U) + AHEAD):
                    if i < len(U):
                        softmax(i)
                    if i >= AHEAD:
                        probs_out(i - AHEAD)
                    if i in (per + AHEAD + 4, 2 * per + AHEAD + 4):
                        merge(KINDS[(i - AHEAD - 4) // per - 1])
                    if i == 2 * per + AHEAD + 7:
                        for j in range(2):
                            src = read(act, "pool", L, j)
                            a(mixT[:, 6 + j, 0:nq], src[:, 0:nq], ACT.Copy, scale=vecT[:, 70 + 2 * L + j:71 + 2 * L + j])\
                                .then_inc(*mark(S, ("read", "pool", L, j), *([("mixT_some", L)] if j else [])))
                act.wait_ge(*at("dsum", L))
                q = nq // P
                a(dstat[:, 0:q, 4:8], dstat[:, 0:q, 0:4], ACT.Ln, scale=1.0 / 64, bias=C("eps")).then_inc(*mark(S, ("dln", L)))
                act.wait_ge(*at("dln", L))
                a(dstat[:, 0:q, 8:12], dstat[:, 0:q, 4:8], ACT.Exp, scale=-0.5).then_inc(*mark(S, ("drstd", L)))
                merge("diff")

            def project_out(L):
                S = f"act_out{L}"
                act.wait_ge(*at("amp", L, 1))
                for what, span, *rest in out_plan(L):
                    lo, hi = span
                    if what == "sum":
                        m, = rest
                        src = read(act, "oT", L, lo, m)[:, 0:SEQ]
                        square(S, ("o", L, span), m, src, SEQ, m % 2)
                        a(oT[:, m, lo:hi], src, ACT.Copy, scale=amp[L][:, 1, m, lo // SEQ:lo // SEQ + 1])\
                            .then_inc(*mark(S, ("read", "oT", L, lo, m)))
                    elif what == "add":
                        finish_rstd(S, ("o", L, span), KD - 1, span, D, ("ckvn", L))
                    elif what == "norm":
                        norm(L, 2, span, ("x_t", L, span, KD - 1))
                    elif what == "h":
                        modulate(L, 2, span)
                    elif what == "logits":
                        copy(S, lgT[0:20, lo:hi], ("lgT", L, lo), SEQ, hi=20, keys=[("lgT", L)] if hi == q_tokens(L) else [])

            def route(L):
                S, nt = f"act_route{L}", q_tokens(L) // P
                for tt in range(nt):
                    for half in range(2):
                        copy(S, rows[:, tt, half * 512:half * 512 + 512], ("hr", L, tt, half),
                             keys=[("h_tile", L, tt)] if half else [])
                if L == DEPTH - 1:
                    for tt in range(nt):
                        for half in range(2):
                            copy(S, x_tok[:, tt, half * 512:half * 512 + 512], ("xr", tt, half), keys=[("x_tok", tt, half)])
                act.wait_ge(*at("g_shift", L))
                a(r4[:, 1, 0:nt, :], r4[:, 0, 0:nt, :], ACT.Exp).then_inc(*mark(S, ("g_exp", L)))
                act.wait_ge(*at("top_diff", L))
                a(rs[:, 7, 0:nt], rs[:, 6, 0:nt], ACT.Exp).then_inc(*mark(S, ("top_exp", L)))
                if L == DEPTH - 1:
                    for half in range(2):
                        copy(S, amp_row[:, half * 512:half * 512 + 512], ("amp_row", half), keys=[("amp_row", half)])

            def experts(L):
                gu_done, silu_ready = sem(f"gu_done{L}"), sem(f"silu_ready{L}")
                act_turned, actT_ready, y_done = sem(f"act_turned{L}"), sem(f"actT_ready{L}"), sem(f"y_done{L}")
                y_copied = sem(f"y_copied{L}")

                def silu(g):
                    act.wait_ge(gu_done, g + 1)
                    a(silu_g, psum[:, 1, 0:256], ACT.Silu).then_inc(silu_ready, 1)

                def actT_out(g):
                    act.wait_ge(act_turned, g + 1)
                    a(actT[:, :, :].rearrange("p c s -> p (c s)"), psum[:, 2, 0:256], ACT.Copy).then_inc(actT_ready, 1)

                def y_out(n, par):
                    act.wait_ge(y_done, n)
                    act.wait_ge(sem(f"y_stored{par}{L}"), ((n + 1) >> 1) * 32)
                    a(y_sb[par], psum[:, 3, :], ACT.Copy).then_inc(y_copied, 1)
                    act.wait_ge(y_copied, n)
                    for j in range(2):
                        act.dma_start(y_rows[ds(n * BLK - BLK, BLK), j * 512:(j + 1) * 512], y_sb[par][64 * j:64 * j + 64, :])\
                            .then_inc(sem(f"y_stored{par}{L}"), 16)

                act.wait_ge(*at("tab", L))
                act.wait_ge(*at("y_zero", 1))
                for par in range(2):
                    act.sem_inc(sem(f"y_stored{par}{L}"), 32)
                total = act.value_load(tabs[L][0:1, T_TOTAL:T_TOTAL + 1], min_val=N_EXP, max_val=MAXBLK)
                silu(0)
                actT_out(0)
                silu(1)
                y_out(1, 0)
                actT_out(1)
                with act.Fori(1, (total + 1) >> 1) as pair:
                    for par in range(2):
                        g = pair * 2 + par
                        silu(g)
                        y_out(g, 1 - par)
                        actT_out(g)
                with act.If((total & 1) < 1):
                    y_out(total, 1)
                act.sem_inc(sem("hold_act"), 1)

            def combine(L):
                S, nt = f"act_comb{L}", q_tokens(L) // P
                for tt in range(nt):
                    act.wait_ge(*at("y_sum", L, tt))
                    a(yb[:, tt, :], ya[tt], ACT.Square, accum_out=rs[:, 20, tt:tt + 1]).then_inc(*mark(S, ("y_sq", L, tt)))
                    act.wait_ge(*at("y_sq", L, tt))
                    a(rs[:, 21, tt:tt + 1], rs[:, 20, tt:tt + 1], ACT.Ln, scale=1.0 / D, bias=C("eps")).then_inc(*mark(S, ("y_ln", L, tt)))
                    act.wait_ge(*at("y_ln", L, tt))
                    a(rs[:, 22, tt:tt + 1], rs[:, 21, tt:tt + 1], ACT.Exp, scale=-0.5).then_inc(*mark(S, ("y_rstd", L, tt)))

            act.preload_act_table_set(LN_EXP)
            with nc.allow_non_contiguous_dma(reason="small vectors"):
                act.dma_start(c_sb[:, 0, :], A["c"].rearrange("o (p k) -> p (o k)", p=P)).then_inc(*mark("dma_c", by=16))
                act.dma_start(c_sb[:, 1, :], A["c_ctx"].rearrange("(p k) -> p k", p=P)).then_inc(*mark("dma_c", ("c",), by=16))
                lo, hi = CST["soon"]
                act.dma_start(cst[:, lo:hi], A["constants"][:, lo:hi]).then_inc(*mark("dma_soon", ("soon",), by=16))
                for i, (lo, src) in enumerate([
                        (0, A["norm_g"].rearrange("l i (k p) -> (l i k) p", p=P)),
                        (64, A["mla_q_gain"].rearrange("l (k p) -> (l k) p", p=P)),
                        (68, A["mla_kv_gain"]),
                        (70, A["pool_scale"].rearrange("l (k p) -> (l k) p", p=P))]):
                    act.dma_start(vec_rows[lo:lo + src.shape[0], :], src).then_inc(*mark("dma_vec", by=16))
                act.dma_start(bias_rows[0:96, :], A["ada_b"].rearrange("l (m p) -> (l m) p", p=P))\
                    .then_inc(*mark("dma_vec", ("vec_rows",), by=16))

                def small_weights(L, S):
                    act.dma_start(w_uq[:, :, :], A["mla_w_uq"][L].rearrange("(j p) n -> p j n", p=P)).then_inc(*mark(S, by=16))
                    act.dma_start(w_ukv[:, :], A["mla_w_ukv"][L]).then_inc(*mark(S, by=16))
                    act.dma_start(w_rt[:, :, 0:4], A["router_gw"][L].rearrange("(k p) n -> p k n", p=P)).then_inc(*mark(S, by=16))
                    act.dma_start(w_rt[:, :, 4:20], A["router_ew"][L].rearrange("(k p) n -> p k n", p=P)).then_inc(*mark(S, by=16))
                    act.wait_ge(*at("pads"))
                    for g in range(4):
                        lo = 64 * (g % 2)
                        act.dma_start(w_pool[lo:lo + 64, g // 2, lo:lo + 64], A["pool_w"][L, g])\
                            .then_inc(*mark(S, *([("small_w", L)] if g == 3 else []), by=16))

            def rest_of_loads():
                with nc.allow_non_contiguous_dma(reason="small vectors"):
                    _, lo = CST["soon"]
                    act.wait_ge(*at("staged", item_no[("in", 0, 0)]))
                    act.dma_start(cst[:, lo:], A["constants"][:, lo:]).then_inc(*mark("dma_const", ("const",), by=16))
                    small_weights(0, "dma_small0")
                    for L in range(DEPTH):
                        for dst, src in ((rt_b[:, L, 0:4], A["router_gb"][L]), (rt_b[:, L, 4:20], A["router_eb"][L]),
                                         (neg_sink[:, L * 4:L * 4 + 4], A["swa_sink"][L]),
                                         (dl[:, L, :, :].rearrange("p a b -> p (a b)"), A["diff_lambda"][L].rearrange("a b -> (a b)")),
                                         (subln[:, L, :], A["diff_subln"][L])):
                            act.dma_start(dst, src.partition_broadcast(P)).then_inc(*mark("dma_rows", by=16))
                        M.name("dma_rows", ("rows", L))

            act.wait_ge(*at("c"))
            a(c_t[:, :, :], c_sb[:, :, :], ACT.Exp, scale=-1.0).then_inc(*mark("act_start", ("c_exp",)))
            for k in range(KD):
                copy("act_start", xT[:, k, :], ("x0", k))
            for L in range(DEPTH):
                for span in spans(L, 1):
                    norm(L, 1, span, ("xn", L - 1, 2, span, KD - 1) if L else None)
                    modulate(L, 1, span)
                if L == 0:
                    rest_of_loads()
                project(L)
                latent_projections(L)
                if L == 0:
                    act.wait_ge(*at("lam_dots"))
                    a(dlp[:, :, :, 0:1].rearrange("p a b c -> p (a b c)"), dls[:, :], ACT.Exp).then_inc(*mark("act_lam", ("lam_exp",)))
                mix(L)
                project_out(L)
                route(L)
                if L == 0:
                    act.wait_ge(*at("filled", "rk", 0))
                    with nc.allow_non_contiguous_dma(reason="small weights"):
                        small_weights(1, "dma_small1")
                act.preload_act_table(ACT.Silu)
                experts(L)
                act.preload_act_table_set(LN_EXP)
                combine(L)

        @block.vector
        def _(v):
            tt_, ts, stt = nc.vector.tensor_tensor, nc.vector.tensor_scalar, nc.vector.scalar_tensor_tensor
            red = nc.vector.tensor_reduce

            def norm(L, w, span):
                lo, hi = span
                v.wait_ge(*at("rstd", (L, w, span)))
                for k in range(KD):
                    tt_(hT[:, k, lo:hi], xT[:, k, lo:hi], rstd[:, lo:hi], ALU.mult)\
                        .then_inc(*mark(f"v_norm{w}{L}{lo}", ("xn", L, w, span, k)))

            def ada_rows(S, L, r):
                v.wait_ge(*at("used", item_no[("ada", L, 4 * r + 3)]))
                if (L, r) != (0, 0):
                    v.wait_ge(*at("filled", "adaT", *((L, r - 1) if r else (L - 1, 2))))
                nc.vector.tensor_copy(ada_sb[:, :], psum[:, B_ADA, :]).then_inc(*mark(S, ("ada_sb", L, r)))

            def ada_columns(S, L, r):
                t = read(v, "adaT", L, r).rearrange("p (q g c) -> p q g c", q=4, g=4)
                for q in range(4):
                    dst = mod[L][:, r * 16:(r + 1) * 16, :].rearrange("p (g q) s -> p q g s", q=4)[:, q, :, :]
                    b = ada_bT[:, L * 48 + r * 16:L * 48 + (r + 1) * 16].rearrange("p (g q) -> p q g", q=4)[:, q, :]
                    ins = tt_(dst, t[:, q, :, 0:2], b.unsqueeze(2).to_broadcast([P, 4, 2]), ALU.add)
                ins.then_inc(*mark(S, ("read", "adaT", L, r)))
                v.wait_ge(*at("read", "adaT", L, r))

                def gains(i):
                    return vecT[:, L * 32 + i * 8:L * 32 + i * 8 + 8].unsqueeze(2).to_broadcast([P, 8, 2])

                if r == 0:
                    stt(amp[L][:, 0, :, :], mod[L][:, 8:16, :], 1.0, gains(0), ALU.add, ALU.mult).then_inc(*mark(S, ("amp", L, 0)))
                elif r == 1:
                    tt_(amp[L][:, 1, :, :], mod[L][:, 16:24, :], gains(1), ALU.mult).then_inc(*mark(S, ("amp", L, 1)))
                else:
                    tt_(amp[L][:, 3, :, :], mod[L][:, 40:48, :], gains(3), ALU.mult)
                    stt(amp[L][:, 2, :, :], mod[L][:, 32:40, :], 1.0, gains(2), ALU.add, ALU.mult).then_inc(*mark(S, ("amp", L, 2)))

            roped = []

            def rope(S, L, name):
                x, kind, lo, hi = ROPES[L][name]
                i = len(roped) % 2
                roped.append((L, name))
                t = read(v, "rot", L, name)[lo:hi, 0:SEQ]
                tt_(rope_s[i][lo:hi, :], t, C("sin_" + kind)[lo:hi, :], ALU.mult).then_inc(*mark(S, ("read", "rot", L, name)))
                v.wait_ge(*at("read", "rot", L, name))
                v.wait_ge(*at("x_cos", L, name))
                tt_(x, rope_c[i][lo:hi, :], rope_s[i][lo:hi, :], ALU.add).then_inc(*mark(S, ("roped", L, name)))

            def latents(L):
                S, nq = f"v_lat{L}", q_tokens(L)
                v.wait_ge(*at("rstd", ("cq", L)))
                for j in range(2):
                    stt(cq[:, j, 0:nq], cq[:, j, 0:nq], vecT[:, 64 + 2 * L + j:65 + 2 * L + j], rstd[:, 0:nq], ALU.mult, ALU.mult)\
                        .then_inc(*mark(S, *([("cqn", L)] if j else [])))
                v.wait_ge(*at("rstd", ("ckv", L)))
                stt(ckv, ckv, vecT[:, 68 + L:69 + L], rstd[:, :], ALU.mult, ALU.mult).then_inc(*mark(S, ("ckvn", L)))
                rope(S, L, "kr")
                v.wait_ge(*at("roped", L, "kr"))
                for h in range(HEADS):
                    nc.vector.tensor_copy(kas[L][64:96, h, :], kr[64:96, :]).then_inc(*mark(S, ("kr_out", L, h)))
                for name in ("bk", "bq0", "bq1", "qa0", "qa1", "qa2", "qa3"):
                    rope(S, L, name)

            def rope_late(S, L, name):
                rope(S, L, name)
                if name[:2] == "dq":
                    j, nq = int(name[2]), q_tokens(L)
                    v.wait_ge(*at("roped", L, name))
                    ts(dqs[L][:, j, 1, 0:nq], dqs[L][:, j, 0, 0:nq], C("parity")[:, 1:2], None, ALU.mult).then_inc(*mark(S, ("dq_odd", L, j)))
                    ts(dqs[L][:, j, 0, 0:nq], dqs[L][:, j, 0, 0:nq], C("parity")[:, 0:1], None, ALU.mult).then_inc(*mark(S, ("dq_split", L, j)))

            def mix(L):
                S = f"v_mix{L}"
                U, nq = units(L), q_tokens(L)
                per = len(U) // 3
                ada = ada_plan(L)

                def maxima(u):
                    kind, qt, h = U[u]
                    nk = NTOK if qt < 2 else SEQ
                    s_ = st[:, u % 8, :]
                    if u >= 8:
                        v.wait_ge(*at("read", "s", L, u - 8, 1 if U[u - 8][0] == "diff" else 0))
                        if U[u - 8][0] == "swa":
                            v.wait_ge(*at("sink", L, u - 8))
                    for j in range(2 if kind == "diff" else 1):
                        ins = red(s_[:, j:j + 1], read(v, "s", L, u, j)[:, 0:nk], AX.X, ALU.max, negate=True)
                    if kind == "swa":
                        ins.then_inc(*mark(S, ("smax", L, u)))
                        v.wait_ge(*at("smax", L, u))
                        ins = tt_(s_[:, 0:1], s_[:, 0:1], neg_sink[:, L * 4 + h:L * 4 + h + 1], ALU.min)
                    ins.then_inc(*mark(S, ("nmax", L, u)))

                def weigh(u):
                    kind, qt, h = U[u]
                    nk = NTOK if qt < 2 else SEQ
                    s_ = st[:, u % 8, :]
                    v.wait_ge(*at("read", "s", L, u, 1 if kind == "diff" else 0))
                    if kind == "swa":
                        v.wait_ge(*at("sink", L, u))
                        tt_(s_[:, 2:3], s_[:, 2:3], s_[:, 4:5], ALU.add).then_inc(*mark(S, ("denom", L, u)))
                        v.wait_ge(*at("denom", L, u))
                    if kind == "diff":
                        nc.vector.reciprocal(s_[:, 5:6], s_[:, 3:4]).then_inc(*mark(S, ("r1", L, u)))
                        v.wait_ge(*at("r1", L, u))
                        stt(s_[:, 6:7], s_[:, 2:3], s_[:, 5:6], neg_lam[:, L:L + 1], ALU.mult, ALU.mult).then_inc(*mark(S, ("c1", L, u)))
                        v.wait_ge(*at("c1", L, u))
                        stt(prob[u % (AHEAD + 1)][:, 0:nk], prob2[:, 0:nk], s_[:, 6:7], prob[u % (AHEAD + 1)][:, 0:nk], ALU.mult, ALU.add)\
                            .then_inc(*mark(S, ("prob", L, u)))
                    nc.vector.reciprocal(s_[:, 7:8], s_[:, 2:3]).then_inc(*mark(S, ("rinv", L, u)))

                def outputs(u):
                    kind, qt, h = U[u]
                    o_ = om[KINDS.index(kind) % 2]
                    keys = [("om", L, kind)] if u % per == per - 1 and kind != "diff" else []
                    if kind == "diff" and u % per == 0:
                        v.wait_ge(*at("filled", "mT", L, "mla", 1))
                    t = read(v, "o", L, u)
                    v.wait_ge(*at("rinv", L, u))
                    ts(o_[:, qt, h * 64:h * 64 + 64], t[:, 0:64], st[:, u % 8, 7:8], None, ALU.mult)\
                        .then_inc(*mark(S, ("read", "o", L, u), *keys))

                done = 0
                for i in range(len(U) + AHEAD + 2):
                    if i < len(U):
                        maxima(i)
                    if 1 <= i < len(U) + 1:
                        weigh(i - 1)
                    if i >= AHEAD + 2:
                        outputs(i - AHEAD - 2)
                    if i in ROPED_LATE:
                        rope_late(S, L, ROPED_LATE[i])
                    while done < len(ada) and done * len(U) <= (i - 1) * len(ada):
                        _, la, ia = ada[done]
                        if ia % 4 == 3:
                            ada_rows(S, la, ia // 4)
                        if ia % 4 == 1 and (la, ia) != (0, 5):
                            ada_columns(S, *((la, ia // 4 - 1) if ia // 4 else (la - 1, 2)))
                        done += 1
                if ada:
                    assert done == len(ada)
                    ada_columns(S, 1, 2)
                q = nq // P
                o_ = om[0][:, 0:q, :]
                v.wait_ge(*at("read", "o", L, len(U) - 1))
                v.wait_ge(*at("filled", "mT", L, "swa", 1))
                tmp = om[1][:, 0:q, :]
                tt_(tmp, o_, o_, ALU.mult).then_inc(*mark(S, ("osq", L)))
                v.wait_ge(*at("osq", L))
                red(dstat[:, 0:q, 0:4], tmp.rearrange("p q (h c) -> p q h c", h=HEADS), AX.X, ALU.add).then_inc(*mark(S, ("dsum", L)))
                v.wait_ge(*at("drstd", L))
                for i in range(q):
                    tt_(o_[:, i, :].rearrange("p (h c) -> p h c", h=HEADS), o_[:, i, :].rearrange("p (h c) -> p h c", h=HEADS),
                        dstat[:, i, 8:12].unsqueeze(2).to_broadcast([P, HEADS, 64]), ALU.mult).then_inc(*mark(S, ("on", L, i)))
                for i in range(q):
                    v.wait_ge(*at("on", L, i))
                    ins = tt_(o_[:, i, :].rearrange("p (h c) -> p h c", h=HEADS), o_[:, i, :].rearrange("p (h c) -> p h c", h=HEADS),
                              subln[:, L, :].unsqueeze(1).to_broadcast([P, HEADS, 64]), ALU.mult)
                ins.then_inc(*mark(S, ("om", L, "diff")))

            def add_out(L):
                S = f"v_out{L}"
                for what, span, *rest in out_plan(L):
                    lo, hi = span
                    if what == "add":
                        v.wait_ge(*at("rstd", ("o", L, span)))
                        for k in range(KD):
                            v.wait_ge(*at("read", "oT", L, lo, k))
                            tt_(oT[:, k, lo:hi], oT[:, k, lo:hi], rstd[:, lo:hi], ALU.mult).then_inc(*mark(S, ("x_t", L, span, k)))
                        for k in range(KD):
                            v.wait_ge(*at("x_t", L, span, k))
                            tt_(xT[:, k, lo:hi], xT[:, k, lo:hi], oT[:, k, lo:hi], ALU.add).then_inc(*mark(S, ("x", L, 1, span, k)))
                    elif what == "h":
                        norm(L, 2, span)

            def route(L):
                S, nt = f"v_route{L}", q_tokens(L) // P
                n = [0]

                def step(ins, *keys):
                    n[0] += 1
                    ins.then_inc(*mark(S, ("step", L, n[0]), *keys))
                    v.wait_ge(*at("step", L, n[0]))

                def b4(x):
                    return x.unsqueeze(2).to_broadcast([P, nt, 4])

                def s1(i):
                    return rs[:, i, 0:nt]

                first = C("first").unsqueeze(1).to_broadcast([P, nt, 4])

                def first_max(x, top, out_, tmp):
                    step(tt_(tmp, x, b4(top), ALU.is_equal))
                    step(tt_(tmp, tmp, first, ALU.mult))
                    step(red(s1(30), tmp, AX.X, ALU.max))
                    step(tt_(out_, tmp, b4(s1(30)), ALU.is_equal))

                t = read(v, "lg", L)[:, 0:nt * 20].rearrange("p (t c) -> p t c", t=nt)
                step(tt_(lg[:, 0:nt, :], t, rt_b[:, L, :].unsqueeze(1).to_broadcast([P, nt, 20]), ALU.add), ("read", "lg", L))
                g_, e_ = lg[:, 0:nt, 0:4], lg[:, 0:nt, 4:20].rearrange("p t (g j) -> p t g j", g=4)
                R4 = [r4[:, i, 0:nt, :] for i in range(10)]
                step(red(s1(0), g_, AX.X, ALU.max))
                step(tt_(R4[0], g_, b4(s1(0)), ALU.subtract), ("g_shift", L))
                first_max(g_, s1(0), R4[2], R4[3])
                m = r16[:, 5, 0:nt, :].rearrange("p t (g j) -> p t g j", g=4)
                step(tt_(m, e_, R4[2].unsqueeze(3).to_broadcast([P, nt, 4, 4]), ALU.mult))
                step(red(R4[4], m.rearrange("p t g j -> p t j g"), AX.X, ALU.add))
                step(red(s1(1), R4[4], AX.X, ALU.max))
                first_max(R4[4], s1(1), R4[5], R4[3])
                step(stt(R4[6], R4[5], NEG, R4[4], ALU.mult, ALU.add))
                step(red(s1(2), R4[6], AX.X, ALU.max))
                step(tt_(s1(6), s1(2), s1(1), ALU.subtract), ("top_diff", L))
                first_max(R4[6], s1(2), R4[7], R4[3])
                for which, oh in ((0, R4[5]), (1, R4[7])):
                    step(tt_(r16[:, which, 0:nt, :].rearrange("p t (g j) -> p t g j", g=4),
                             R4[2].unsqueeze(3).to_broadcast([P, nt, 4, 4]), oh.unsqueeze(2).to_broadcast([P, nt, 4, 4]), ALU.mult))
                step(tt_(chosen[:, 4 - nt:4, :], r16[:, 0, 0:nt, :], r16[:, 1, 0:nt, :], ALU.add), ("chosen", L))
                v.wait_ge(*at("g_exp", L))
                step(red(s1(3), R4[1], AX.X, ALU.add))
                step(nc.vector.reciprocal(s1(4), s1(3)))
                v.wait_ge(*at("top_exp", L))
                step(ts(s1(5), s1(7), 1.0, None, ALU.add))
                step(nc.vector.reciprocal(s1(8), s1(5)))
                step(tt_(s1(9), s1(8), s1(4), ALU.mult))
                step(tt_(s1(10), s1(9), s1(7), ALU.mult), ("weights", L))
                t = read(v, "rk", L)
                step(nc.vector.tensor_copy(e16[:, 0, :], t[:, nt * 16:nt * 16 + 16]))
                step(tt_(cmp7[:, :, :], e16[:, 0, :].unsqueeze(2).to_broadcast([P, 16, 7]),
                         C("more").unsqueeze(1).to_broadcast([P, 16, 7]), ALU.is_ge))
                step(red(e16[:, 1, :], cmp7[:, :, :], AX.X, ALU.add))
                step(ts(e16[:, 1, :], e16[:, 1, :], 1.0, None, ALU.add))
                step(nc.vector.tensor_tensor_scan(e16[:, 2, :], ones[:, 0:16], e16[:, 1, :], 0.0, ALU.mult, ALU.add))
                step(tt_(e16[:, 3, :], e16[:, 2, :], e16[:, 1, :], ALU.subtract))
                step(ts(e16[:, 4, :], e16[:, 3, :], float(BLK), None, ALU.mult))
                step(tt_(r16[:, 3, 0:nt, :], t[:, 0:nt * 16].rearrange("p (t e) -> p t e", t=nt),
                         e16[:, 4, :].unsqueeze(1).to_broadcast([P, nt, 16]), ALU.add), ("read", "rk", L))
                for which in range(2):
                    step(tt_(r16[:, 4, 0:nt, :], r16[:, 3, 0:nt, :], r16[:, which, 0:nt, :], ALU.mult))
                    step(red(s1(11 + which), r16[:, 4, 0:nt, :], AX.X, ALU.add))
                step(nc.vector.tensor_copy(spos[:, 0:2 * nt].rearrange("p (w t) -> p w t", w=2), rs[:, 11:13, 0:nt]), ("spos", L))
                n2 = 2 * nt
                ts(spos_t[:, 0, 0:n2], spos[:, 0:n2], BLK - 1, None, ALU.bitwise_and)
                step(ts(spos_t[:, 1, 0:n2], spos[:, 0:n2], 6, None, ALU.logical_shift_right))
                step(nc.vector.tensor_copy(spos_f[:, :, 0:n2], spos_t[:, :, 0:n2]))
                tt_(place_hot[:, 0:n2, :], spos_f[:, 0, 0:n2].unsqueeze(2).to_broadcast([P, n2, BLK]),
                    C("count")[:, 0:BLK].unsqueeze(1).to_broadcast([P, n2, BLK]), ALU.is_equal)
                step(tt_(block_id[:, 0:n2, :], spos_f[:, 1, 0:n2].unsqueeze(2).to_broadcast([P, n2, COLS]),
                         C("count")[:, 0:COLS].unsqueeze(1).to_broadcast([P, n2, COLS]), ALU.is_equal))
                step(tt_(block_id[:, 0:n2, :], block_id[:, 0:n2, :], C(f"token{L}").unsqueeze(2).to_broadcast([P, n2, COLS]), ALU.mult),
                     ("slot_hot", L))
                for off, i in ((T_NB, 1), (T_START, 3), (T_CUM, 2)):
                    nc.vector.tensor_copy(tabs[L][:, off:off + 16], e16[:, i, :])
                step(nc.vector.tensor_copy(tabs[L][:, T_TOTAL:T_TOTAL + 1], e16[:, 2, 15:16]), ("tab", L))
                t = read(v, "st", L)
                nc.vector.tensor_copy(slots[:, :], t[0:BLK, 0:COLS]).then_inc(*mark(S, ("read", "st", L), ("slots", L)))
                if L == DEPTH - 1:
                    v.wait_ge(*at("sq_used", (L, 2, (0, SEQ)), KD - 1))
                    for k in range(KD):
                        ins = ts(sq[k // 4][:, k % 4 * P:(k % 4 + 1) * P], ident, amp[L][:, 3, k, 0:1], None, ALU.mult)
                        if k % 4 == 3:
                            ins.then_inc(*mark(S, ("diagonal", k // 4)))

            def experts(L):
                x_turned, x_ready = sem(f"x_turned{L}"), sem(f"x_ready{L}")
                silu_ready, act_ready = sem(f"silu_ready{L}"), sem(f"act_ready{L}")

                def x_out():
                    return nc.vector.tensor_copy(xgT[:, :, :].rearrange("p k s -> p (k s)"), psum[:, 0, :]).then_inc(x_ready, 1)

                total = v.value_load(tabs[L][0:1, T_TOTAL:T_TOTAL + 1], min_val=N_EXP, max_val=MAXBLK)
                v.wait_ge(x_turned, 1)
                x_out()
                with v.Fori(0, (total + 1) >> 1) as pair:
                    for par in range(2):
                        g = pair * 2 + par
                        v.wait_ge(silu_ready, g + 1)
                        tt_(act_rows, silu_g, psum[:, 1, 256:512], ALU.mult).then_inc(act_ready, 1)
                        v.wait_ge(x_turned, g + 2)
                        x_out()
                v.wait_ge(x_ready, ((total + 1) >> 1) * 2 + 1)
                nc.vector.memset(rs[:, 31, 0:1], 0.0).then_inc(*mark(f"v_comb{L}", ("banks_out", L)))

            def combine(L):
                S, nt = f"v_comb{L}", q_tokens(L) // P

                def add(tt):
                    v.wait_ge(*at("ya", L, tt))
                    ts(ya[tt], ya[tt], rs[:, 9, tt:tt + 1], None, ALU.mult).then_inc(*mark(S, ("y1", L, tt)))
                    v.wait_ge(*at("y1", L, tt))
                    v.wait_ge(*at("yb", L, tt))
                    stt(ya[tt], yb[:, tt, :], rs[:, 10, tt:tt + 1], ya[tt], ALU.mult, ALU.add).then_inc(*mark(S, ("y_sum", L, tt)))

                def scale(tt):
                    v.wait_ge(*at("y_rstd", L, tt))
                    ts(ya[tt], ya[tt], rs[:, 22, tt:tt + 1], None, ALU.mult).then_inc(*mark(S, ("y_norm", L, tt)))

                def add_to_x(span):
                    lo, hi = span
                    for k in range(KD):
                        t = read(v, "yT", L, lo, k // 2)
                        ins = stt(xT[:, k, lo:hi], t[:, k % 2 * SEQ:(k % 2 + 1) * SEQ], amp[L][:, 3, k, lo // SEQ:lo // SEQ + 1],
                                  xT[:, k, lo:hi], ALU.mult, ALU.add)
                        ins.then_inc(*mark(S, ("x", L, 2, span, k), *([("read", "yT", L, lo, k // 2)] if k % 2 else [])))

                if L == 0:
                    first, second = spans(1, 1)
                    for tt in range(3):
                        add(tt)
                    for tt in range(2):
                        scale(tt)
                    add(3)
                    add_to_x(first)
                    for tt in range(2, 4):
                        scale(tt)
                    norm(1, 1, first)
                    add_to_x(second)
                    norm(1, 1, second)
                    return
                for tt in range(nt):
                    add(tt)
                v.wait_ge(*at("x_tok", nt - 1, 1))
                v.wait_ge(*at("amp_row", 1))
                for tt in range(nt):
                    v.wait_ge(*at("y_rstd", L, tt))
                    stt(ya[tt], ya[tt], rs[:, 22, tt:tt + 1], amp_row, ALU.mult, ALU.mult).then_inc(*mark(S, ("y_norm", L, tt)))
                    v.wait_ge(*at("y_norm", L, tt))
                    tt_(ya[tt], ya[tt], x_tok[:, tt, :], ALU.add).then_inc(*mark(S, ("result", tt)))

            def shared_rows():
                S = "v_rows"
                v.wait_ge(*at("rows", DEPTH - 1))
                ts(neg_sink[:, :], neg_sink[:, :], -1.0, None, ALU.mult)
                for L in range(DEPTH):
                    ts(subln[:, L, :], subln[:, L, :], 1.0 - LAM_INIT[L], None, ALU.mult)
                d = dl[:, :, :, :].rearrange("p l (a b) c -> p l a b c", b=2)
                for L in range(DEPTH):
                    ins = tt_(dlp[:, L, :, :], d[:, L, :, 0, :], d[:, L, :, 1, :], ALU.mult)
                ins.then_inc(*mark(S, ("lam_prod",)))
                v.wait_ge(*at("lam_prod"))
                red(dls[:, :], dlp[:, :, :, :].rearrange("p l a c -> p (l a) c"), AX.X, ALU.add).then_inc(*mark(S, ("lam_dots",)))
                v.wait_ge(*at("lam_exp"))
                for L in range(DEPTH):
                    ins = stt(neg_lam[:, L:L + 1], dlp[:, L, 1, 0:1], -LAM_INIT[L], dlp[:, L, 0, 0:1], ALU.add, ALU.subtract)
                ins.then_inc(*mark(S, ("neg_lam",)))

            S0 = "v_start"
            nc.vector.memset(ones[:, :], 1.0).then_inc(*mark(S0, ("ones",)))
            for j in range(2):
                nc.vector.memset(up[j][:, :, :], 0.0)
            nc.vector.memset(w_pool[:, :, :], 0.0).then_inc(*mark(S0, ("pads",)))
            nc.vector.memset(silu_c[:, :, :], 0.0).then_inc(*mark(S0, ("silu_zero",)))
            nc.vector.memset(chosen[:, :, :], 0.0)
            t = read(v, "vec")
            nc.vector.tensor_copy(vecT[:, :], t[:, 0:74])
            nc.vector.tensor_copy(ada_bT[:, :], t[:, P:P + 96]).then_inc(*mark(S0, ("read", "vec")))
            v.wait_ge(*at("c_exp"))
            ts(c_t[:, :, :], c_t[:, :, :], 1.0, None, ALU.add).then_inc(*mark(S0, ("c1",)))
            v.wait_ge(*at("c1"))
            nc.vector.reciprocal(c_t[:, :, :], c_t[:, :, :]).then_inc(*mark(S0, ("c2",)))
            v.wait_ge(*at("c2"))
            v.wait_ge(*at("silu_zero"))
            tt_(silu_c[:, :, 0:2].rearrange("p k s -> p s k"), c_sb[:, :, :], c_t[:, :, :], ALU.mult).then_inc(*mark(S0, ("silu_c",)))
            norm(0, 1, (0, NTOK))
            ada_rows(S0, 0, 0)
            ada_columns(S0, 0, 0)
            v.wait_ge(*at("const"))
            nc.vector.tensor_copy(band[:, :], C("band"))
            nc.vector.tensor_copy(ident16[:, :], ident).then_inc(*mark("v_band", ("band",)))
            for L in range(DEPTH):
                latents(L)
                if L == 0:
                    shared_rows()
                mix(L)
                add_out(L)
                route(L)
                experts(L)
                combine(L)

        @block.gpsimd
        def _(g_):
            gt = nc.gpsimd.tensor_tensor

            def cosines(L):
                S = f"g_rope{L}"
                order = ["kr", "bk", "bq0", "bq1", "qa0", "qa1", "qa2", "qa3", "dq0", "dk0", "dq1", "dk1"]
                for n, name in enumerate(order):
                    x, kind, lo, hi = ROPES[L][name]
                    g_.wait_ge(*at("tile", L, name))
                    if n:
                        g_.wait_ge(*at("x_cos", L, order[n - 1]))
                    if n >= 2:
                        g_.wait_ge(*at("roped", L, order[n - 2]))
                    gt(rope_c[n % 2][lo:hi, :], x, C("cos_" + kind)[lo:hi, :], ALU.mult).then_inc(*mark(S, ("x_cos", L, name)))

            def pooling(L, j):
                S, ns = f"g_pool{L}", q_tokens(L) // SEQ
                n = [0]

                def step(ins, *keys):
                    n[0] += 1
                    ins.then_inc(*mark(S, ("pstep", L, j, n[0]), *keys))
                    g_.wait_ge(*at("pstep", L, j, n[0]))

                def widen(dst, src, lo, hi, half, r=0):
                    step(gt(dst[r:, 0:ns, lo:hi], src[r:, 0:ns, lo - half:hi - half], src[r:, 0:ns, lo + half:hi + half], ALU.add))

                g_.wait_ge(*at("read", f"u{j}", L))
                if j == 0:
                    g_.wait_ge(*at("x_cos", L, "dk1"))
                step(gt(pa[:, 0:ns, 1:PADW], up[j][:, 0:ns, 0:PADW - 1], up[j][:, 0:ns, 1:PADW], ALU.add))
                if j == 0:
                    widen(pb, pa, 2, PADW - 2, 1, 64)
                else:
                    widen(pb, pa, 2, PADW - 2, 1)
                    widen(pa, pb, 4, PADW - 4, 2)
                    widen(pb, pa, 8, PADW - 8, 4, 64)
                d = dgs[L][:, j, :].rearrange("p (s t) -> p s t", s=2)
                for r, src in ((0, pa), (64, pb)):
                    for s in range(ns):
                        step(gt(d[r:r + 64, s, :], src[r:r + 64, s, 16:16 + SEQ], inv_count[r:r + 64, j, :], ALU.mult))
                step(gt(d[:, 0:ns, :], d[:, 0:ns, :], up[j][:, 0:ns, 16:16 + SEQ], ALU.subtract), ("dg", L, j))

            def route(L):
                S, nt = f"g_route{L}", q_tokens(L) // P
                for tt in range(nt):
                    g_.wait_ge(*at("h_tile", L, tt))
                    g_.dma_start(h_rows[L][tt * P:(tt + 1) * P, :], rows[:, tt, :]).then_inc(*mark(f"dma_h{L}", ("h_stored", L, tt), by=16))

            def experts(L):
                x_rows, x_turned, col_ready = sem(f"x_rows{L}"), sem(f"x_turned{L}"), sem(f"col_ready{L}")
                g_.wait_ge(*at("slots", L))
                g_.wait_ge(*at("h_stored", L, q_tokens(L) // P - 1))

                def gather(g, par, to):
                    nc.gpsimd.tensor_copy(slot_col[:, par:par + 1], slots[:, ds(g, 1)]).then_inc(col_ready, 1)
                    g_.wait_ge(col_ready, g + 1)
                    g_.sem_inc(sem("hold"), 1)
                    g_.indirect_dma_start(to, None, h_rows[L], bass.IndirectOffsetOnAxis(ap=slot_col[:, par:par + 1], axis=0))\
                        .then_inc(sem(f"gathered{par}{L}"), 16)

                def pass_on(g, par):
                    g_.wait_ge(sem(f"gathered{par}{L}"), ((g >> 1) + 1) * 16)
                    if not isinstance(g, int) or g:
                        g_.wait_ge(x_turned, g)
                    g_.sem_inc(sem("hold"), 1)
                    nc.gpsimd.tensor_copy(xg, xg_in[par]).then_inc(x_rows, 1)
                    g_.wait_ge(x_rows, g + 1)

                gather(0, 0, xg)
                gather(1, 1, xg_in[1])
                g_.wait_ge(*at("tab", L))
                total = g_.value_load(tabs[L][0:1, T_TOTAL:T_TOTAL + 1], min_val=N_EXP, max_val=MAXBLK)
                pairs = (total >> 1) + 1
                g_.wait_ge(sem(f"gathered0{L}"), 16)
                g_.sem_inc(x_rows, 1)
                gather(2, 0, xg_in[0])
                pass_on(1, 1)
                gather(3, 1, xg_in[1])
                with g_.Fori(1, pairs - 1) as pair:
                    for par in range(2):
                        pass_on(pair * 2 + par, par)
                        gather(pair * 2 + (par + 2), par, xg_in[par])
                pass_on(pairs * 2 - 2, 0)
                pass_on(pairs * 2 - 1, 1)
                for par in range(2):
                    g_.wait_ge(sem(f"y_stored{par}{L}"), ((total + (1 - par)) >> 1) * 32 + 32)
                g_.wait_ge(sem(f"actT_ready{L}"), ((total + 1) >> 1) * 2)
                g_.sem_inc(sem("hold"), 1)
                g_.wait_ge(*at("banks_out", L))
                for tt in range(q_tokens(L) // P):
                    for which, dst in ((0, ya[tt]), (1, yb[:, tt, :])):
                        g_.indirect_dma_start(dst, None, y_rows,
                                              bass.IndirectOffsetOnAxis(ap=spos[:, which * (q_tokens(L) // P) + tt:which * (q_tokens(L) // P) + tt + 1], axis=0))\
                            .then_inc(*mark(f"dma_y{L}{tt}{which}", ("yb" if which else "ya", L, tt), by=16))

            nc.gpsimd.memset(zeros[:, :], 0.0).then_inc(*mark("g_start", ("zeros",)))
            g_.wait_ge(*at("zeros"))
            g_.wait_ge(*at("staged", item_no[("in", 0, 3)]))
            for half in range(2):
                g_.dma_start(y_rows.rearrange("(p n) (h d) -> p n h d", p=P, h=2)[:, :, half, :],
                             zeros[:, :].unsqueeze(1).to_broadcast([P, y_rows.shape[0] // P, D // 2]))\
                    .then_inc(*mark("dma_y_zero", ("y_zero", half), by=16))
            g_.wait_ge(*at("const"))
            for L in range(DEPTH):
                cosines(L)
                pooling(L, 0)
                pooling(L, 1)
                route(L)
                experts(L)

        @block.sync
        def _(sp):
            def load(n):
                it = items[n]
                buf = buffers[n]
                if buf in buffers[:n] and n != n_stage0 + buf:
                    last = max(i for i in range(n) if buffers[i] == buf)
                    sp.wait_ge(*at("used", last))
                dst = staged(it) if it[0] != "ada" else stage[buf].rearrange("p (k c) -> p k c", k=2)
                sp.dma_start(dst, stage_source(it)).then_inc(*mark(f"dma_stage{buf}", ("staged", n), by=16))

            PIECES = {"lo": "lo_done", "hi": "gu_done", "dn": "y_done"}

            def load_piece(L, e, par, piece):
                gu = A["exp_w_gu"][L].rearrange("e (k p) n -> e p k n", p=P)
                dn = A["exp_w_down"][L].rearrange("e (k p) n -> e p k n", p=P)

                def pick(x):
                    return x[e] if isinstance(e, int) else x[ds(e, 1), :, :, :].squeeze(0)

                place = (par + L) % 2
                if piece == "lo":
                    sp.dma_start(w_gu_in[place][:, 0:4, :], pick(gu)[:, 0:4, :]).then_inc(sem(f"w_lo{place}"), 16)
                elif piece == "hi":
                    sp.dma_start(w_gu_in[place][:, 4:8, :], pick(gu)[:, 4:8, :]).then_inc(sem(f"w_hi{place}"), 16)
                else:
                    sp.dma_start(w_dn[place], pick(dn)).then_inc(sem(f"w_dn{place}"), 16)

            sp.dma_start(rows[:, 0:2, :], A["x"][0].rearrange("(t p) d -> p t d", p=P)).then_inc(*mark("dma_x", by=16))
            sp.dma_start(rows[:, 2:4, :], A["ctx"][0].rearrange("(t p) d -> p t d", p=P)).then_inc(*mark("dma_x", ("x_rows",), by=16))
            load(0)
            sp.wait_ge(*at("vec_rows"))
            for L in range(DEPTH):
                lo, hi = (1, n_stage0) if L == 0 else (n_stage0, len(items))
                if L:
                    cum = sp.value_load(tabs[L - 1][0:1, T_CUM + N_EXP - 2:T_CUM + N_EXP - 1], min_val=1, max_val=MAXBLK)
                    for n, done in enumerate(("lo_done", "gu_done")):
                        sp.wait_ge(sem(f"{done}{L - 1}"), cum)
                        sp.sem_inc(sem("sp_hold"), 1)
                        load(lo + n)
                    lo += 2
                    sp.wait_ge(*at("yb", L - 1, q_tokens(L - 1) // P - 1))
                for n in range(lo, hi):
                    load(n)
                sp.wait_ge(*at("filled", "mT", L, "diff", 1))
                sp.wait_ge(*at("filled", "pool", L, 1))
                for piece in PIECES:
                    load_piece(L, 0, 0, piece)
                for n in (hi - 2, hi - 1):
                    sp.wait_ge(*at("used", n))
                for piece in PIECES:
                    load_piece(L, 1, 1, piece)
                sp.wait_ge(*at("filled", *(("xr", 1, 1) if L else ("hr", L, 3, 1))))
                dn = A["exp_w_down"][L, 2].rearrange("(k p) n -> p k n", p=P)
                for k in range(4):
                    sp.dma_start(w_dn_ahead[L][k], dn[:, k, :]).then_inc(*mark(f"dma_ahead{L}", *([("ahead", L)] if k == 3 else []), by=16))
                sp.wait_ge(*at("tab", L))

                def next_expert(pair, par):
                    cum = sp.value_load(tabs[L][0:1, ds(pair * 2 + (T_CUM - 2 + par), 1)], min_val=1, max_val=MAXBLK)
                    for piece, done in PIECES.items():
                        if piece == "dn" and isinstance(pair, int) and par == 0:
                            break
                        sp.wait_ge(sem(f"{done}{L}"), cum)
                        load_piece(L, pair * 2 + par, par, piece)

                next_expert(1, 0)
                next_expert(1, 1)
                with sp.Fori(2, N_EXP // 2) as pair:
                    next_expert(pair, 0)
                    next_expert(pair, 1)
            for tt in range(2):
                sp.wait_ge(*at("result", tt))
                sp.dma_start(out[0, tt * P:(tt + 1) * P, :], ya[tt]).then_inc(*mark("dma_out", by=16))
            sp.wait_ge(sem("dma_out"), 32)
        return M


_INS = ['x', 'c', 'ctx', 'c_ctx', 'ada_w', 'ada_b', 'norm_g', 'w_in', 'mla_q_gain', 'mla_kv_gain', 'mla_w_uq',
        'mla_w_ukv', 'swa_sink', 'diff_lambda', 'diff_subln', 'pool_w', 'pool_scale', 'w_out', 'router_gw',
        'router_gb', 'router_ew', 'router_eb', 'exp_w_gu', 'exp_w_down']


def kernel(**inputs):
    import numpy as _np
    import concourse.bacc as _bacc
    from concourse import mybir as _mybir
    from concourse.bass_utils import run_bass_kernel_spmd as _run

    arrays = {f"in_{name}_dram": _np.ascontiguousarray(inputs[name]) for name in _INS}
    arrays["in_constants_dram"] = CONSTANTS

    def build(known):
        nc = _bacc.Bacc("TRN2", target_bir_lowering=False, num_devices=1)
        args = {n[3:-5]: nc.dram_tensor(n, a.shape, _mybir.dt.from_np(a.dtype), kind="ExternalInput").ap()
                for n, a in arrays.items()}
        out = nc.dram_tensor("out_0_dram", (1, SEQ, D), _mybir.dt.float32, kind="ExternalOutput").ap()
        return nc, hybrid_block(nc, args, out, known)

    _, counts = build(None)
    nc, _ = build(counts)
    r = _run(nc, [arrays], core_ids=[0])
    return r.results[0]["out_0_dram"]
```
